# Optimizing a Trainium2 kernel written in Bass

```python
import jax, jax.numpy as jnp
from jax import lax
import numpy as np

D_MODEL = 2048
BATCH = 1
SEQ = 256
DEPTH = 2

GRID_W = 64
CTX_LEN = 256
N_MIXERS = 2
MIXER_MLA = 0
MIXER_FOURIER = 1
N_MLA_LAYERS = (DEPTH + 1) // 2
N_FNO_LAYERS = DEPTH // 2
N_HEADS = 16
Q_LORA = 512
KV_LORA = 512
QK_NOPE = 128
QK_ROPE = 64
V_DIM = 128
ROPE_BASE = 10000.0
Q_BLOCK = 128
SM_SCALE = (QK_NOPE + QK_ROPE) ** -0.5
FNO_GROUPS = 8
FNO_GROUP_DIM = D_MODEL // FNO_GROUPS
D_FF = 5632
CONV_W = 3
NORM_EPS = 1e-6
N_MOD = 6

kernel_name = "hybrid_mla_fnet_convffn_dit"

def _rmsnorm(x, g):
    xf = x.astype(jnp.float32)
    y = xf * lax.rsqrt(jnp.mean(xf * xf, axis=-1, keepdims=True) + NORM_EPS)
    return (y * g.astype(jnp.float32)).astype(x.dtype)

def _ada(cond, w, b):
    m = jax.nn.silu(cond) @ w + b
    m = m.reshape(m.shape[:-1] + (N_MOD, D_MODEL))
    return jnp.split(m, N_MOD, axis=-2)

def _modulate(h, shift, scale):
    return h * (1 + scale) + shift

def _axial_rope_tables(n, dtype):
    rows = n // GRID_W
    r, col = jnp.meshgrid(jnp.arange(rows, dtype=jnp.float32),
                          jnp.arange(GRID_W, dtype=jnp.float32), indexing="ij")
    r = r.reshape(-1)
    col = col.reshape(-1)
    half = QK_ROPE // 2
    inv_freq = jnp.power(ROPE_BASE, -jnp.arange(0, half, 2, dtype=jnp.float32) / half)
    ang_r = r[:, None] * inv_freq
    ang_c = col[:, None] * inv_freq
    ang = jnp.concatenate([ang_r, ang_r, ang_c, ang_c], axis=-1)
    return jnp.cos(ang).astype(dtype), jnp.sin(ang).astype(dtype)

def _rotate_axial(u):
    half = QK_ROPE // 2
    q = half // 2
    a1, a2 = u[..., :q], u[..., q:half]
    b1, b2 = u[..., half:half + q], u[..., half + q:]
    return jnp.concatenate([-a2, a1, -b2, b1], axis=-1)

def _apply_rope(u, cos, sin):
    return u * cos + _rotate_axial(u) * sin

def _mla_down(h, w_dqkv):
    d = h @ w_dqkv
    return d[..., :Q_LORA], d[..., Q_LORA:Q_LORA + KV_LORA], d[..., Q_LORA + KV_LORA:]

def _mla_queries(c_q, g_q, w_uq):
    b, n, _ = c_q.shape
    q = (_rmsnorm(c_q, g_q) @ w_uq).reshape(b, n, N_HEADS, QK_NOPE + QK_ROPE)
    return q[..., :QK_NOPE], q[..., QK_NOPE:]

def _mla_keys(c_kv, g_kv, w_ukv):
    b, n, _ = c_kv.shape
    kv = (_rmsnorm(c_kv, g_kv) @ w_ukv).reshape(b, n, N_HEADS, QK_NOPE + V_DIM)
    return kv[..., :QK_NOPE], kv[..., QK_NOPE:]

def _attend(qn, qr, kn, kr, v):
    s = jnp.einsum("bqhd,bkhd->bhqk", qn, kn) + jnp.einsum("bqhr,bkr->bhqk", qr, kr)
    p = jax.nn.softmax(s.astype(jnp.float32) * SM_SCALE, axis=-1).astype(v.dtype)
    return jnp.einsum("bhqk,bkhd->bqhd", p, v)

def _mla(hx, hc, w_dqkv, g_q, g_kv, w_uq, w_ukv, w_o, cos, sin, ctx_out):
    b, n, _ = hx.shape
    cq_x, ckv_x, kr_x = _mla_down(hx, w_dqkv)
    qn_x, qr_x = _mla_queries(cq_x, g_q, w_uq)
    qr_x = _apply_rope(qr_x, cos[None, :, None, :], sin[None, :, None, :])
    kn_x, v_x = _mla_keys(ckv_x, g_kv, w_ukv)
    kr_x = _apply_rope(kr_x, cos[None], sin[None])
    cq_c, ckv_c, kr_c = _mla_down(hc, w_dqkv)
    kn_c, v_c = _mla_keys(ckv_c, g_kv, w_ukv)
    kn = jnp.concatenate([kn_c, kn_x], axis=1)
    kr = jnp.concatenate([kr_c, kr_x], axis=1)
    v = jnp.concatenate([v_c, v_x], axis=1)
    nb = n // Q_BLOCK

    def to_blocks(t):
        return jnp.moveaxis(t.reshape((b, nb, Q_BLOCK) + t.shape[2:]), 1, 0)

    def block(qs):
        qn_b, qr_b = qs
        return _attend(qn_b, qr_b, kn, kr, v)

    o = lax.map(block, (to_blocks(qn_x), to_blocks(qr_x)))
    o = jnp.moveaxis(o, 0, 1).reshape(b, n, N_HEADS * V_DIM)
    yx = o @ w_o
    yc = None
    if ctx_out:
        qn_c, qr_c = _mla_queries(cq_c, g_q, w_uq)
        oc = _attend(qn_c, qr_c, kn_c, kr_c, v_c)
        yc = oc.reshape(b, hc.shape[1], N_HEADS * V_DIM) @ w_o
    return yx, yc

def _fourier_mix(h, w):
    b, n, _ = h.shape
    hg = h.astype(jnp.float32).reshape(b, n, FNO_GROUPS, FNO_GROUP_DIM)
    f = jnp.fft.fft2(hg, axes=(1, 3), norm="ortho").real
    return f.reshape(b, n, D_MODEL).astype(h.dtype) @ w

def _dwconv3(u, w, bias):
    up = jnp.pad(u, ((0, 0), (1, 1), (0, 0)))
    return up[:, :-2] * w[0] + up[:, 1:-1] * w[1] + up[:, 2:] * w[2] + bias

def _conv_ffn(h, w_up, conv_w, conv_b, w_down):
    u = _dwconv3(h @ w_up, conv_w, conv_b)
    val, gate = jnp.split(u, 2, axis=-1)
    return (val * jax.nn.silu(gate)) @ w_down

def setup_inputs(seed: int = 0) -> dict:
    key = jax.random.key(seed)
    ks = jax.random.split(key, 20)
    nrm = jax.random.normal
    f32 = jnp.float32
    D = D_MODEL
    return {
        "x": nrm(ks[0], (BATCH, SEQ, D), f32),
        "c": nrm(ks[1], (BATCH, D), f32),
        "ctx": nrm(ks[2], (BATCH, CTX_LEN, D), f32),
        "c_ctx": nrm(ks[3], (D,), f32),
        "ada_w": nrm(ks[4], (DEPTH, D, N_MOD * D), f32) * D ** -0.5,
        "ada_b": nrm(ks[5], (DEPTH, N_MOD * D), f32) * 0.02,
        "norm1_g": 1.0 + 0.02 * nrm(ks[6], (DEPTH, D), f32),
        "norm2_g": 1.0 + 0.02 * nrm(ks[7], (DEPTH, D), f32),
        "mla_w_dqkv": nrm(ks[8], (N_MLA_LAYERS, D, Q_LORA + KV_LORA + QK_ROPE), f32) * D ** -0.5,
        "mla_q_norm_g": 1.0 + 0.02 * nrm(ks[9], (N_MLA_LAYERS, Q_LORA), f32),
        "mla_kv_norm_g": 1.0 + 0.02 * nrm(ks[10], (N_MLA_LAYERS, KV_LORA), f32),
        "mla_w_uq": nrm(ks[11], (N_MLA_LAYERS, Q_LORA, N_HEADS * (QK_NOPE + QK_ROPE)), f32) * Q_LORA ** -0.5,
        "mla_w_ukv": nrm(ks[12], (N_MLA_LAYERS, KV_LORA, N_HEADS * (QK_NOPE + V_DIM)), f32) * KV_LORA ** -0.5,
        "mla_w_o": nrm(ks[13], (N_MLA_LAYERS, N_HEADS * V_DIM, D), f32) * (N_HEADS * V_DIM) ** -0.5,
        "fno_w": nrm(ks[14], (N_FNO_LAYERS, D, D), f32) * D ** -0.5,
        "ffn_w_up": nrm(ks[15], (DEPTH, D, 2 * D_FF), f32) * D ** -0.5,
        "ffn_conv_w": nrm(ks[16], (DEPTH, CONV_W, 2 * D_FF), f32) * CONV_W ** -0.5,
        "ffn_conv_b": nrm(ks[17], (DEPTH, 2 * D_FF), f32) * 0.02,
        "ffn_w_down": nrm(ks[18], (DEPTH, D_FF, D), f32) * D_FF ** -0.5,
        "final_norm_g": 1.0 + 0.02 * nrm(ks[19], (D,), f32),
    }

def reference(x, c, ctx, c_ctx, ada_w, ada_b, norm1_g, norm2_g, mla_w_dqkv, mla_q_norm_g,
              mla_kv_norm_g, mla_w_uq, mla_w_ukv, mla_w_o, fno_w, ffn_w_up, ffn_conv_w,
              ffn_conv_b, ffn_w_down, final_norm_g):
    n = x.shape[1]
    cos, sin = _axial_rope_tables(n, x.dtype)
    for i in range(DEPTH):
        kind = i % N_MIXERS
        j = i // N_MIXERS
        ctx_later = any(l % N_MIXERS == MIXER_MLA for l in range(i + 1, DEPTH))
        sh1, sc1, g1, sh2, sc2, g2 = _ada(c, ada_w[i], ada_b[i])
        hx = _modulate(_rmsnorm(x, norm1_g[i]), sh1, sc1)
        hc = None
        if kind == MIXER_MLA or ctx_later:
            csh1, csc1, cg1, csh2, csc2, cg2 = _ada(c_ctx, ada_w[i], ada_b[i])
            hc = _modulate(_rmsnorm(ctx, norm1_g[i]), csh1, csc1)
        if kind == MIXER_MLA:
            yx, yc = _mla(hx, hc, mla_w_dqkv[j], mla_q_norm_g[j], mla_kv_norm_g[j], mla_w_uq[j],
                          mla_w_ukv[j], mla_w_o[j], cos, sin, ctx_later)
        else:
            yx = _fourier_mix(hx, fno_w[j])
            yc = _fourier_mix(hc, fno_w[j]) if ctx_later else None
        x = x + g1 * yx
        x = x + g2 * _conv_ffn(_modulate(_rmsnorm(x, norm2_g[i]), sh2, sc2),
                               ffn_w_up[i], ffn_conv_w[i], ffn_conv_b[i], ffn_w_down[i])
        if ctx_later:
            ctx = ctx + cg1 * yc
            ctx = ctx + cg2 * _conv_ffn(_modulate(_rmsnorm(ctx, norm2_g[i]), csh2, csc2),
                                        ffn_w_up[i], ffn_conv_w[i], ffn_conv_b[i], ffn_w_down[i])
    return _rmsnorm(x, final_norm_g)


_drawn_inputs = setup_inputs


def setup_inputs(seed=0):
    import zlib

    import numpy as np

    out = dict(_drawn_inputs(seed))
    spreads = {}
    factors = {'norm1_g': 6.941,
     'norm2_g': 2.841,
     'mla_q_norm_g': 8.0,
     'mla_kv_norm_g': 8.0,
     'ffn_conv_b': 3.589,
     'final_norm_g': 2.922}
    for name, (base, spread) in spreads.items():
        noise = np.random.default_rng([zlib.crc32(name.encode()), seed]).standard_normal(out[name].shape)
        drawn = base * np.exp(spread * noise) if base else spread * noise
        out[name] = __import__('jax').numpy.asarray(drawn.astype(out[name].dtype))
    for name, factor in factors.items():
        out[name] = (out[name] * factor).astype(out[name].dtype)
    return out
```

```python
from contextlib import ExitStack

import numpy as np
import concourse.bass as bass
from concourse import mybir

P = 128
D = 2048
KT = D // P
SEQ = 256
NTOK = 2 * SEQ
HEADS = 16
LORA = 512
LT = LORA // P
ROPE = 64
VD = 128
SM_SCALE = (128 + ROPE) ** -0.5
EPS = 1e-6
D_FF = 5632
FT = D_FF // P
PARTS = (32, 12)
UNIT = P
CH = 8 * UNIT
RING = 4
GRID_W = 64

C_DQKV = 0
N_DQKV = 2 * 9
C_HEAD = C_DQKV + N_DQKV
N_HEAD = 2 * HEADS
C_WO = C_HEAD + N_HEAD
C_FFN0 = C_WO + 2 * KT
N_FFN = FT * 4 + FT * KT // 8
C_FNO = C_FFN0 + N_FFN
C_FFN1 = C_FNO + 2 * KT
N_CHUNKS = C_FFN1 + N_FFN

SH1, SC1, G1, SH2, SC2, G2 = range(6)
ADA_BLOCKS = [(G1, 1), (SC2, 1), (SH2, 1), (G2, 2), (6 + SC1, 2), (6 + SH2, 1), (6 + SC2, 1), (6 + G2, 1)]
ADA_AT = [0]
ADA_ACCS = [0]
for _first, _n in ADA_BLOCKS:
    ADA_AT.append(ADA_AT[-1] + 32 * _n)
    ADA_ACCS.append(ADA_ACCS[-1] + _n)
N_ADA = ADA_AT[-1]
MODS_EARLY = 2
N_EARLY = 64


def backbone(nc, xT, ctxT, cond, ada_early, ada_late, ada_b, gains, lat_gains, weights, conv, consts, rope,
             dft, outT):
    f32, f32r = mybir.dt.float32, mybir.dt.float32r
    ALU, ACT, AX = mybir.AluOpType, mybir.ActivationFunctionType, mybir.AxisListType
    es = ExitStack()
    with es:
        base = -(-nc.sbuf_base // 64) * 64
        room = nc.sbuf_usable_end - base
        es.enter_context(nc.sbuf_tensor("arena", [P, (room - 64) // 4], f32))
        cursor = [0]

        def at(name, shape, dtype, offset):
            return nc.alloc_sbuf_tensor_at(name, shape, dtype, offset=base + offset)

        def place(name, shape, dtype=f32):
            offset = cursor[0]
            cursor[0] += -(-4 * int(np.prod(shape[1:])) // 32) * 32
            assert cursor[0] <= room - 64, (name, cursor[0], room)
            return at(name, shape, dtype, offset)

        x = place("x", [P, KT, SEQ])
        h_hi = place("h_hi", [P, KT, SEQ], f32r)
        h_at = cursor[0]
        h_lo = place("h_lo", [P, KT, SEQ], f32r)
        h_pre = at("h_pre", [P, KT, SEQ], f32, h_at)
        raw = place("raw", [P, RING, CH])
        w_hi = place("w_hi", [P, RING, CH], f32r)
        w_lo = place("w_lo", [P, RING, CH], f32r)
        ada = place("ada", [P, RING, CH])
        acc0 = place("acc0", [P, D])
        rs_at = cursor[0]
        rstd = place("rstd", [P, NTOK])
        sq = place("sq", [P, NTOK])
        sqt_at = cursor[0]
        sqt = place("sqt", [P, 2, SEQ])
        conv_at = cursor[0]
        conv_s = place("conv_s", [P, 2 * FT, 4])
        const_s = place("const_s", [P, 2, P])
        mod = place("mod", [P, 12, KT])
        mod_c = place("mod_c", [P, 2, KT])
        bias_s = place("bias_s", [P, 12, KT])
        gain_s = place("gain_s", [P, 5, KT])
        lgain_s = place("lgain_s", [P, 2, LT])
        scl = place("scl", [P, 5, KT])
        cond_s = place("cond_s", [P, KT, 2])
        silu_c = place("silu_c", [P, KT, 2])
        mx = place("mx", [P, 2])
        negmax = place("negmax", [P, 2])
        psum_row = place("psum_row", [P, 2])
        rinv = place("rinv", [P, 2])
        ident, ones = const_s[:, 0, :], const_s[:, 1, :]
        phase_at = cursor[0]

        ckv_hi = place("ckv_hi", [P, LT, NTOK], f32r)
        o = cursor[0]
        ckv_lo = place("ckv_lo", [P, LT, NTOK], f32r)
        ckv = at("ckv", [P, LT, NTOK], f32, o)
        cq_hi = place("cq_hi", [P, LT, SEQ], f32r)
        o = cursor[0]
        cq_lo = place("cq_lo", [P, LT, SEQ], f32r)
        cq = at("cq", [P, LT, SEQ], f32, o)
        kr_hi = place("kr_hi", [P, 2, NTOK], f32r)
        kr_lo = place("kr_lo", [P, 2, NTOK], f32r)
        heads_at = cursor[0]
        qn_hi = place("qn_hi", [P, 2, SEQ], f32r)
        qn_lo = place("qn_lo", [P, 2, SEQ], f32r)
        kn_hi = place("kn_hi", [P, 2, NTOK], f32r)
        kn_lo = place("kn_lo", [P, 2, NTOK], f32r)
        v_hi = place("v_hi", [P, 2, 4, 2 * VD], f32r)
        v_lo = place("v_lo", [P, 2, 4, 2 * VD], f32r)
        qr_hi = place("qr_hi", [P, 2, SEQ], f32r)
        qr_lo = place("qr_lo", [P, 2, SEQ], f32r)
        pt_at = cursor[0]
        pt_hi = place("pt_hi", [P, 4, SEQ], f32r)
        pt_lo = place("pt_lo", [P, 4, SEQ], f32r)
        rope_s = place("rope_s", [P, 2 * SEQ + P])
        cos, sin, rot = rope_s[:, 0:SEQ], rope_s[:, SEQ:2 * SEQ], rope_s[:, 2 * SEQ:]
        hc_hi = at("hc_hi", [P, KT, SEQ], f32r, heads_at)
        ctx_sq = at("ctx_sq", [P, KT, SEQ], f32, heads_at)
        hc_lo = at("hc_lo", [P, KT, SEQ], f32r, heads_at + 4 * KT * SEQ)
        ctx_s = at("ctx_s", [P, KT, SEQ], f32, heads_at + 4 * KT * SEQ)
        kro = at("kro", [P, NTOK], f32, pt_at + 2048)
        krt = at("krt", [P, SEQ], f32, pt_at + 4096)
        assert heads_at + 8 * KT * SEQ <= pt_at + 2048
        prob = at("prob", [P, 2, NTOK], f32, rs_at)
        qraw = at("qraw", [P, SEQ], f32, sqt_at)
        tq = at("tq", [P, SEQ], f32, sqt_at + 4 * SEQ)
        diag = at("diag", [P, 2, P], f32, conv_at)

        cursor[0] = phase_at
        a_hi = place("a_hi", [P, PARTS[0], SEQ], f32r)
        a_lo = place("a_lo", [P, PARTS[0], SEQ], f32r)
        cv = place("cv", [P, 2, 2, SEQ])
        ga = at("ga", [P, SEQ], f32, rs_at + 12 * SEQ)
        acc1 = place("acc1", [P, D])
        cursor[0] = phase_at
        dft_hi = place("dft_hi", [P, 2, 3 * SEQ], f32r)
        o = cursor[0]
        dft_lo = place("dft_lo", [P, 2, 3 * SEQ], f32r)
        dft_s = at("dft_s", [P, 2, 3 * SEQ], f32, o)
        ab_hi = place("ab_hi", [P, 2, 2, 2 * SEQ], f32r)
        ab_lo = place("ab_lo", [P, 2, 2, 2 * SEQ], f32r)
        f_hi = place("f_hi", [P, KT, SEQ], f32r)
        f_lo = place("f_lo", [P, KT, SEQ], f32r)

        bank = [es.enter_context(nc.psum_tensor(f"bank{i}", [P, 512], f32)) for i in range(8)]
        sem = lambda name: es.enter_context(nc.semaphore(name))
        raw_in = [sem(f"raw_in{s}") for s in range(RING)]
        ada_in = [sem(f"ada_in{s}") for s in range(RING)]
        cond_in, x_in, ctx_in, small_in, conv_in, dft_in = (
            sem(n) for n in ("cond_in", "x_in", "ctx_in", "small_in", "conv_in", "dft_in"))
        stored = sem("stored")
        hi_done, lo_done, chunk_used = sem("hi_done"), sem("lo_done"), sem("chunk_used")
        silu_c_done, ada_used_pe, ada_used = sem("silu_c_done"), sem("ada_used_pe"), sem("ada_used")
        acc_zeroed, ada_summed, mod_done, scl_done = (
            sem("acc_zeroed"), sem("ada_summed"), sem("mod_done"), sem("scl_done"))
        sq_done, sqt_done, norm_summed, var_done, std_done, rstd_done = (
            sem(n) for n in ("sq_done", "sqt_done", "norm_summed", "var_done", "std_done", "rstd_done"))
        sq0_done, xr_done = sem("sq0_done"), sem("xr_done")
        pre_done, h_hi_done, h_ready = sem("pre_done"), sem("h_hi_done"), sem("h_ready")
        lat_pre, lat_hi, lat_ready = sem("lat_pre"), sem("lat_hi"), sem("lat_ready")
        kr_rot, kr_step, kr_hi_done, kr_ready, kr_zero = (
            sem("kr_rot"), sem("kr_step"), sem("kr_hi_done"), sem("kr_ready"), sem("kr_zero"))
        tile_done, tile_taken, y_done, y_free = sem("tile_done"), sem("tile_taken"), sem("y_done"), sem("y_free")
        proj_done, proj_taken, kq_hi, v_hi_done, rope_step, qr_hi_done, qr_ready = (
            sem(n) for n in ("proj_done", "proj_taken", "kq_hi", "v_hi_done", "rope_step", "qr_hi_done", "qr_ready"))
        s_done, mx_done, negmax_done, exp_done, rinv_done, diag_done = (
            sem(n) for n in ("s_done", "mx_done", "negmax_done", "exp_done", "rinv_done", "diag_done"))
        t_done, pt_hi_done, pt_ready, o_done, o_hi_done, o_ready = (
            sem(n) for n in ("t_done", "pt_hi_done", "pt_ready", "o_done", "o_hi_done", "o_ready"))
        mid_done, left_done, silu_done, gated, a_hi_done, a_ready = (
            sem(n) for n in ("mid_done", "left_done", "silu_done", "gated", "a_hi_done", "a_ready"))
        dft_hi_done, dft_ready, ab_done, ab_hi_done, ab_ready, f_hi_done, f_ready = (
            sem(n) for n in ("dft_hi_done", "dft_ready", "ab_done", "ab_hi_done", "ab_ready", "f_hi_done", "f_ready"))

        T_UP0, T_DFT = 14, 14 + 2 * FT
        T_UP1 = T_DFT + KT
        Y_WO, Y_FFN0 = 0, KT
        Y_FNO, Y_FFN1 = Y_FFN0 + 2 * KT, Y_FFN0 + 3 * KT
        NRM_KV, NRM_Q, NRM_L0F, NRM_L1, NRM_L1F, NRM_OUT = 2, 3, 4, 5, 6, 7
        H_L0F, H_L1, H_L1F, H_OUT = 32, 48, 64, 80
        SQ_LAT, SQ_ADDS = 12, 16
        MOD_G2 = (MODS_EARLY + 4, MODS_EARLY + 8)

        def one(ap):
            return ap.rearrange("p o n -> p (o n)")

        def row(t, i):
            return one(t[:, bass.ds(i, 1), :])

        def proj_index(n):
            return 6 + 4 * n

        def proj_at(n):
            return 3 + 2 * n

        def head_chunk(n):
            return C_HEAD + 3 + 2 * n

        block = es.enter_context(nc.Block())

        @block.sync
        def _(sp):
            def load_chunk(c, slot):
                sp.dma_start(raw[:, slot, :], one(weights[bass.ds(c, 1), :, :].rearrange("o p n -> p o n")))\
                    .then_inc(raw_in[slot], 16)

            def follow_split(c, slot):
                if isinstance(c, int) and c + RING >= N_CHUNKS:
                    return
                sp.wait_ge(lo_done, c + 1)
                load_chunk(c + RING, slot)

            def follow_ada(a, slot):
                if isinstance(a, int) and a + RING >= N_ADA:
                    return
                sp.wait_ge(ada_used, a + 1)
                sp.dma_start(ada[:, slot, :], one(ada_late[bass.ds(a + RING, 1), :, :].rearrange("o p n -> p o n")))\
                    .then_inc(ada_in[slot], 16)

            sp.dma_start(cond_s[:, :, :], cond).then_inc(cond_in, 16)
            sp.dma_start(const_s[:, :, :], consts).then_inc(small_in, 16)
            sp.dma_start(gain_s[:, :, :], gains).then_inc(small_in, 16)
            sp.dma_start(lgain_s[:, :, :], lat_gains).then_inc(small_in, 16)
            sp.dma_start(bias_s[:, :, :], ada_b).then_inc(small_in, 16)
            sp.dma_start(rope_s[:, :], rope).then_inc(small_in, 16)
            sp.dma_start(ctx_s[:, :, :], ctxT).then_inc(ctx_in, 16)
            sp.dma_start(x[:, :, :], xT).then_inc(x_in, 16)
            for s in range(RING):
                sp.dma_start(ada[:, s, :], ada_early[s, :, :]).then_inc(ada_in[s], 16)
            with sp.Fori(1, N_EARLY // RING) as i:
                for s in range(RING):
                    sp.wait_ge(ada_used_pe, RING * (i - 1) + s + 1)
                    sp.dma_start(ada[:, s, :], one(ada_early[bass.ds(RING * i + s, 1), :, :].rearrange("o p n -> p o n")))\
                        .then_inc(ada_in[s], 16)
            for s in range(RING):
                load_chunk(s, s)
            for s in range(RING):
                sp.wait_ge(ada_used_pe, N_EARLY - RING + s + 1)
                sp.dma_start(ada[:, s, :], ada_late[s, :, :]).then_inc(ada_in[s], 16)
            for c in range(RING):
                follow_split(c, c % RING)
            a = 0
            for t in range(9):
                for _ in range((5, 4, 2)[(t > 3) + (t > 4)]):
                    follow_ada(a, a % RING)
                    a += 1
                for c in (2 * t + 4, 2 * t + 5):
                    follow_split(c, c % RING)
            for c in (22, 23, 24):
                follow_split(c, c % RING)

            def heads(n0, limit):
                for s in range(4):
                    for e in range(2):
                        follow_ada(ADA_AT[1] + 2 * (n0 + s) + e, (2 * s + e) % RING)
                    for e in range(2):
                        if limit is None or C_HEAD + 7 + 2 * (n0 + s) + e <= limit:
                            follow_split(C_HEAD + 7 + 2 * (n0 + s) + e, (C_HEAD + 7 + 2 * s + e) % RING)

            with sp.Fori(0, 3) as i:
                heads(4 * i, None)
            heads(12, C_WO + 3)
            sp.wait_ge(t_done, 2 * HEADS)
            sp.dma_start(conv_s[:, :, :], conv[0]).then_inc(conv_in, 16)

            def square(c0, a0, loops, limit):
                def body(c, a, top):
                    for t in range(2):
                        for e in range(2):
                            follow_ada(a + 2 * t + e, 2 * t + e)
                        for e in range(2):
                            if top is None or c + 7 + 2 * t + e <= top:
                                follow_split(c + 7 + 2 * t + e, (c0 + 7 + 2 * t + e) % RING)
                for c in (c0 + 4, c0 + 5, c0 + 6):
                    follow_split(c, c % RING)
                with sp.Fori(0, loops) as i:
                    body(c0 + 4 * i, a0 + 4 * i, None)
                body(c0 + 4 * loops, a0 + 4 * loops, limit)

            def ffn(c0, layer):
                for c in (c0 + 4, c0 + 5, c0 + 6):
                    follow_split(c, c % RING)

                def up(c, a):
                    for s in range(2):
                        follow_split(c + 4 * s + 7, (c0 + 7) % RING)
                        if a is not None:
                            for e in range(2):
                                follow_ada(a + 2 * s + e, 2 * s + e)
                        for e in range(1, 4):
                            follow_split(c + 4 * s + 7 + e, (c0 + 7 + e) % RING)

                if layer == 0:
                    with sp.Fori(0, 16) as i:
                        up(c0 + 8 * i, ADA_AT[3] + 4 * i)
                else:
                    with sp.Fori(0, 7) as i:
                        up(c0 + 8 * i, ADA_AT[7] + 4 * i)
                    up(c0 + 56, ADA_AT[7] + 28)
                    with sp.Fori(8, 16) as i:
                        up(c0 + 8 * i, None)
                c1 = c0 + 4 * PARTS[0]
                with sp.Fori(0, 8) as i:
                    for t in range(2):
                        follow_split(c1 + 8 * i + 4 * t + 7, (c1 + 7) % RING)
                        if layer == 0:
                            for e in range(4):
                                follow_ada(ADA_AT[4] + 8 * i + 4 * t + e, e)
                        for e in range(1, 4):
                            follow_split(c1 + 8 * i + 4 * t + 7 + e, (c1 + 7 + e) % RING)
                c2 = c1 + 2 * PARTS[0]
                with sp.Fori(0, PARTS[1] // 2) as i:
                    up(c2 + 8 * i, None)
                c3 = c2 + 4 * PARTS[1]
                for t in range(8):
                    for c in range(c3 + 3 * t + 7, c3 + 3 * t + 10):
                        if c <= min(c3 + 24 + 3, N_CHUNKS - 1):
                            follow_split(c, c % RING)

            square(C_WO, ADA_AT[2], 7, C_FFN0 + 3)
            ffn(C_FFN0, 0)
            sp.wait_ge(y_free, 2 + Y_FNO)
            sp.dma_start(dft_s[:, :, :], dft).then_inc(dft_in, 16)
            sp.dma_start(conv_s[:, :, :], conv[1]).then_inc(conv_in, 16)
            for a in range(ADA_AT[5], ADA_AT[6]):
                follow_ada(a, a % RING)
            square(C_FNO, ADA_AT[6], 7, C_FFN1 + 3)
            ffn(C_FFN1, 1)
            for q in range(4):
                sp.wait_ge(pre_done, H_OUT + 4 * (q + 1))
                sp.dma_start(outT[:, 4 * q:4 * q + 4, :], h_pre[:, 4 * q:4 * q + 4, :]).then_inc(stored, 16)
            sp.wait_ge(stored, 64)

        @block.gpsimd
        def _(pool):
            def zero_accs(b):
                if b:
                    pool.wait_ge(mod_done, MODS_EARLY + b)
                for acc in (acc0, acc1)[:ADA_BLOCKS[b][1]]:
                    pool.memset(acc[:, :], 0.0).then_inc(acc_zeroed, 1)

            zero_accs(0)

            srcs = [(T, ckv[:, T // 2, (T % 2) * SEQ:(T % 2 + 1) * SEQ], sq[:, (T % 2) * SEQ:(T % 2 + 1) * SEQ])
                    for T in range(8)]
            srcs += [(10 + t, cq[:, t, :], sq[:, 0:SEQ]) for t in range(LT)]
            for n, (T, src, dst) in enumerate(srcs):
                pool.wait_ge(tile_taken, T + 1)
                if T == 10:
                    pool.wait_ge(norm_summed, NRM_KV + 1)
                if n >= 2:
                    pool.wait_ge(sq_done, n - 1)
                pool.tensor_tensor(sqt[:, n % 2, :], src, src, ALU.mult).then_inc(sqt_done, 1)
                pool.wait_ge(sqt_done, n + 1)
                if T in (0, 1, 10):
                    pool.tensor_copy(dst, sqt[:, n % 2, :]).then_inc(sq_done, 1)
                else:
                    pool.wait_ge(sq_done, n)
                    pool.tensor_tensor(dst, dst, sqt[:, n % 2, :], ALU.add).then_inc(sq_done, 1)
            zero_accs(1)

            def residual_squares(Y0, round_, after):
                pool.wait_ge(*after)
                pool.memset(sq[:, 0:SEQ], 0.0).then_inc(sqt_done, 1)

                with pool.Fori(0, KT // 2) as i:
                    for s in range(2):
                        n = SQ_LAT + SQ_ADDS * round_ + 2 * i + s
                        pool.wait_ge(y_free, 2 + Y0 + 2 * i + s + 1)
                        pool.wait_ge(sq_done, n - 1)
                        xm = row(x, 2 * i + s)
                        pool.tensor_tensor(sqt[:, s, :], xm, xm, ALU.mult).then_inc(sqt_done, 1)
                        pool.wait_ge(sqt_done, n + 1 + round_ + 1)
                        pool.wait_ge(sq_done, n)
                        pool.tensor_tensor(sq[:, 0:SEQ], sq[:, 0:SEQ], sqt[:, s, :], ALU.add).then_inc(sq_done, 1)

            zero_accs(2)
            residual_squares(Y_WO, 0, (o_ready, HEADS))
            zero_accs(3)
            zero_accs(4)
            residual_squares(Y_FFN0 + KT, 1, (norm_summed, NRM_L0F + 1))
            zero_accs(5)
            zero_accs(6)
            residual_squares(Y_FNO, 2, (norm_summed, NRM_L1 + 1))
            zero_accs(7)
            residual_squares(Y_FFN1 + KT, 3, (norm_summed, NRM_L1F + 1))

        @block.scalar
        def _(act):
            def split(c, rounds):
                slot = rounds % RING
                act.wait_ge(raw_in[slot], 4 * (c - slot) + 16)
                act.wait_ge(chunk_used, c - RING + 1)
                act.copy(w_hi[:, slot, :], raw[:, slot, :]).then_inc(hi_done, 1)

            act.wait_ge(cond_in, 16)
            act.activation(silu_c[:, :, :], cond_s[:, :, :], ACT.Silu).then_inc(silu_c_done, 1)
            act.wait_ge(ctx_in, 16)
            act.activation(ctx_sq[:, :, :], ctx_s[:, :, :], ACT.Square).then_inc(sq0_done, 1)
            act.wait_ge(x_in, 16)
            act.activation(h_pre[:, :, :], x[:, :, :], ACT.Square).then_inc(sq0_done, 1)

            def std(k, cols):
                act.wait_ge(var_done, k)
                act.activation(rstd[:, 0:cols], rstd[:, 0:cols], ACT.Sqrt).then_inc(std_done, 1)

            std(1, NTOK)
            for c in range(RING):
                act.wait_ge(raw_in[c], 16)
                act.copy(w_hi[:, c, :], raw[:, c, :]).then_inc(hi_done, 1)
            for m in range(2 * KT):
                act.wait_ge(pre_done, m + 1)
                dst, src = (hc_hi, ctx_s) if m < KT else (h_hi, h_pre)
                act.copy(dst[:, m % KT, :], src[:, m % KT, :]).then_inc(h_hi_done, 1)
            for t in range(9):
                for c in (2 * t + 4, 2 * t + 5):
                    split(c, c)
                if t == 4:
                    std(2, NTOK)
                if t == 5:
                    for m in range(LT):
                        act.wait_ge(lat_pre, m + 1)
                        act.copy(ckv_hi[:, m, :], ckv[:, m, :]).then_inc(lat_hi, 1)
                if t == 6:
                    act.wait_ge(kr_step, 3)
                    act.copy(kr_hi[0:ROPE, 0, :], kro[0:ROPE, :]).then_inc(kr_hi_done, 1)
                    act.copy(kr_hi[ROPE:P, 1, :], kro[ROPE:P, :]).then_inc(kr_hi_done, 1)
            std(3, SEQ)
            for m in range(LT):
                act.wait_ge(lat_pre, LT + m + 1)
                act.copy(cq_hi[:, m, :], cq[:, m, :]).then_inc(lat_hi, 1)

            def v_evac(buf, n_proj, c):
                for e, after in enumerate(((proj_done, n_proj), (chunk_used, c + 1))):
                    act.wait_ge(*after)
                    act.copy(v_hi[:, buf, 2 * e:2 * e + 2, :], bank[e][:, :].rearrange("p (t n) -> p t n", t=2))\
                        .then_inc(v_hi_done, 1)

            def kq_evac(buf, n_proj, c):
                act.wait_ge(proj_done, n_proj)
                act.copy(kn_hi[:, buf, :], bank[0][:, :]).then_inc(kq_hi, 1)
                act.wait_ge(chunk_used, c + 1)
                act.copy(qn_hi[:, buf, :], bank[1][:, 0:SEQ]).then_inc(kq_hi, 1)

            def qr_evac(p, buf):
                act.wait_ge(rope_step, 3 * p + 3)
                act.copy(qr_hi[:, buf, :], tq[:, :]).then_inc(qr_hi_done, 1)

            v_evac(0, 1, C_HEAD)
            split(22, 22)
            kq_evac(0, 2, C_HEAD + 1)
            split(23, 23)
            qr_evac(0, 0)
            split(24, 24)

            def step(n, s, p, last, top):
                for qt in range(2):
                    act.wait_ge(negmax_done, 2 * n + qt + 1)
                    act.activation(prob[:, qt, :], bank[4 + qt][:, :], ACT.Exp, bias=negmax[:, qt:qt + 1],
                                   scale=SM_SCALE, accum_out=psum_row[:, qt:qt + 1]).then_inc(exp_done, 1)
                if last < 1:
                    kq_evac((s + 1) % 2, proj_at(n) + 1, head_chunk(n))
                c = C_HEAD + 7 + 2 * n
                if top is None or c <= top:
                    split(c, C_HEAD + 7 + 2 * s)
                for qt in range(2):
                    act.wait_ge(t_done, 2 * n + qt + 1)
                    act.copy(pt_hi[:, :, qt * P:(qt + 1) * P], bank[6 + qt][:, :].rearrange("p (t n) -> p t n", t=4))\
                        .then_inc(pt_hi_done, 1)
                if last < 0:
                    if s % 2 == 0:
                        v_evac((s // 2 + 1) % 2, proj_at(n) + 2, head_chunk(n) + 1)
                    else:
                        qr_evac(p, (s // 2 + 1) % 2)
                if top is None or c + 1 <= top:
                    split(c + 1, C_HEAD + 8 + 2 * s)
                act.wait_ge(o_done, n + 1)
                act.copy(row(h_hi, n), bank[3][:, 0:SEQ]).then_inc(o_hi_done, 1)

            with act.Fori(0, 3) as i:
                for s in range(4):
                    step(4 * i + s, s, 2 * i + (s + 1) // 2, -1, None)
            for s in range(4):
                step(12 + s, s, 6 + (s + 1) // 2, (s > 1) + (s > 2) - 1, C_WO + 3)

            def square(c0, loops, limit):
                for c in (c0 + 4, c0 + 5, c0 + 6):
                    split(c, c)
                with act.Fori(0, loops) as i:
                    for e in range(4):
                        split(c0 + 4 * i + 7 + e, c0 + 7 + e)
                for e in range(4):
                    c = c0 + 4 * loops + 7 + e
                    if c <= limit:
                        split(c, c)

            def normed(k, h0, shift):
                std(k, SEQ)
                for m in range(KT):
                    act.wait_ge(pre_done, h0 + m + 1)
                    act.activation(h_hi[:, m, :], h_pre[:, m, :], ACT.Identity, bias=mod[:, shift, m:m + 1])\
                        .then_inc(h_hi_done, 1)

            def ffn(c0, T0, P0, layer):
                for c in (c0 + 4, c0 + 5, c0 + 6):
                    split(c, c)

                def pair(c, T, Pn, f, j, s):
                    split(c + 7, c0 + 7)
                    for g in range(2):
                        act.wait_ge(chunk_used, c + 2 * g + 2)
                        taps = conv_s[:, bass.ds(2 * f + g, 1), :]
                        act.activation(cv[:, s, g, :], bank[(T0 + 2 * s + g) % 4][:, 0:SEQ], ACT.Identity,
                                       bias=taps[:, :, 3], scale=taps[:, :, 1]).then_inc(mid_done, 1)
                    split(c + 8, c0 + 8)
                    act.wait_ge(tile_taken, T + 2)
                    act.activation(cv[:, s, 1, :], cv[:, s, 1, :], ACT.Silu).then_inc(silu_done, 1)
                    act.wait_ge(gated, Pn + 1)
                    act.copy(row(a_hi, j), ga[:, :]).then_inc(a_hi_done, 1)
                    split(c + 9, c0 + 9)
                    split(c + 10, c0 + 10)

                act.wait_ge(conv_in, 16 * (layer + 1))
                with act.Fori(0, PARTS[0] // 2) as i:
                    for s in range(2):
                        j = 2 * i + s
                        pair(c0 + 8 * i + 4 * s, T0 + 4 * i + 2 * s, P0 + j, j, j, s)
                c1 = c0 + 4 * PARTS[0]
                with act.Fori(0, KT // 2) as i:
                    for e in range(8):
                        split(c1 + 8 * i + 7 + e, c1 + 7 + e)
                c2 = c1 + 2 * PARTS[0]
                with act.Fori(0, PARTS[1] // 2) as i:
                    for s in range(2):
                        j = 2 * i + s
                        pair(c2 + 8 * i + 4 * s, T0 + 2 * PARTS[0] + 4 * i + 2 * s, P0 + PARTS[0] + j,
                             PARTS[0] + j, j, s)
                c3 = c2 + 4 * PARTS[1]
                for c in range(c3 + 7, c3 + 24 + 4):
                    if c < N_CHUNKS:
                        split(c, c)

            square(C_WO, 7, C_FFN0 + 3)
            normed(4, H_L0F, SH2)
            ffn(C_FFN0, T_UP0, 0, 0)
            act.wait_ge(dft_in, 16)
            act.copy(dft_hi[:, :, :], dft_s[:, :, :]).then_inc(dft_hi_done, 1)
            normed(5, H_L1, 6 + SH1)

            def spectrum(g):
                for t in range(2):
                    act.wait_ge(ab_done, 2 * g + t + 1)
                    act.copy(ab_hi[:, g % 2, t, :], bank[4 + t][:, :]).then_inc(ab_hi_done, 1)

            def back(g):
                for m in (2 * g, 2 * g + 1):
                    act.wait_ge(tile_done, 5 + m + 1)
                    act.copy(f_hi[:, m, :], bank[(T_DFT + m) % 4][:, 0:SEQ]).then_inc(f_hi_done, 1)

            for g in range(9):
                if g < 8:
                    spectrum(g)
                if g:
                    back(g - 1)
            square(C_FNO, 7, C_FFN1 + 3)
            normed(6, H_L1F, 6 + SH2)
            ffn(C_FFN1, T_UP1, FT, 1)
            std(7, SEQ)

        @block.vector
        def _(dve):
            def split(c, slot):
                dve.wait_ge(hi_done, c + 1)
                dve.tensor_tensor(w_lo[:, slot, :], raw[:, slot, :], w_hi[:, slot, :].bitcast(f32), ALU.subtract)\
                    .then_inc(lo_done, 1)

            def lo_of(dst, src, hi_part, done):
                dve.tensor_tensor(dst, src, hi_part.bitcast(f32), ALU.subtract).then_inc(done, 1)

            def ada_step(b, k, e, a0):
                both = ADA_BLOCKS[b][1] == 2
                width = 4 if both else 2
                a = a0
                slot = e % RING
                dve.wait_ge(ada_in[slot], 4 * (a - slot) + 16 * (N_EARLY // RING + 1))
                if not (isinstance(a, int) and a < width):
                    dve.wait_ge(ada_used, a - width + 1)
                acc = (acc0, acc1)[(e % width) // 2]
                part = acc[:, (e % 2) * CH:(e % 2 + 1) * CH]
                dve.scalar_tensor_tensor(part, ada[:, slot, :], one(silu_c[:, bass.ds(k, 1), 0:1]), part,
                                         ALU.mult, ALU.add).then_inc(ada_used, 1)

            def mods(b):
                first, n = ADA_BLOCKS[b]
                dve.wait_ge(ada_summed, b + 1)
                dve.tensor_tensor(mod[:, first:first + n, :], bank[7][:, 0:n * KT].rearrange("p (n k) -> p n k", n=n),
                                  bias_s[:, first:first + n, :], ALU.add).then_inc(mod_done, 1)

            def scales(i, scale, gain, need):
                dve.wait_ge(mod_done, need)
                dve.scalar_tensor_tensor(scl[:, i, :], scale, 1.0, gain_s[:, gain, :], ALU.add, ALU.mult)\
                    .then_inc(scl_done, 1)

            def invert(k, cols):
                dve.wait_ge(std_done, k)
                dve.reciprocal(rstd[:, 0:cols], rstd[:, 0:cols]).then_inc(rstd_done, 1)
                dve.wait_ge(rstd_done, k)

            dve.memset(mx[:, :], 0.0).then_inc(y_free, 2)
            dve.wait_ge(small_in, 16 * 5)
            dve.wait_ge(norm_summed, 2)
            dve.tensor_scalar(rstd[:, :], bank[6][:, :], 1.0 / D, EPS, ALU.mult, ALU.add).then_inc(var_done, 1)
            invert(1, NTOK)
            for m in range(KT):
                dve.tensor_tensor(ctx_s[:, m, :], ctx_s[:, m, :], rstd[:, 0:SEQ], ALU.mult).then_inc(xr_done, 1)
            for m in range(KT):
                dve.tensor_tensor(h_pre[:, m, :], x[:, m, :], rstd[:, SEQ:NTOK], ALU.mult).then_inc(xr_done, 1)
            dve.wait_ge(ada_used_pe, N_EARLY)
            early = bank[0][:, 0:2 * 2 * KT].rearrange("p (m k s) -> p m k s", m=2, s=2)
            dve.tensor_tensor(mod_c[:, :, :], early[:, :, :, 1], bias_s[:, 0:2, :], ALU.add).then_inc(mod_done, 1)
            dve.tensor_tensor(mod[:, 0:2, :], early[:, :, :, 0], bias_s[:, 0:2, :], ALU.add).then_inc(mod_done, 1)
            scales(1, mod_c[:, SC1, :], 0, MODS_EARLY)
            scales(0, mod[:, SC1, :], 0, MODS_EARLY)
            for c in range(RING):
                split(c, c)
            dve.wait_ge(scl_done, 2)
            dve.wait_ge(xr_done, 2 * KT)

            def first_pre(m):
                src, s, md = (ctx_s, 1, mod_c) if m < KT else (h_pre, 0, mod)
                k = m % KT
                dve.tensor_scalar(src[:, k, :], src[:, k, :], scl[:, s, k:k + 1], md[:, SH1, k:k + 1],
                                  ALU.mult, ALU.add).then_inc(pre_done, 1)

            def first_lo(m):
                dst, src, hi_part = (hc_lo, ctx_s, hc_hi) if m < KT else (h_lo, h_pre, h_hi)
                dve.wait_ge(h_hi_done, m + 1)
                lo_of(dst[:, m % KT, :], src[:, m % KT, :], hi_part[:, m % KT, :], h_ready)

            for m in range(2 * KT + 2):
                if m < 2 * KT:
                    first_pre(m)
                if m >= 2:
                    first_lo(m - 2)

            a = 0
            for t in range(9):
                if t < 5:
                    for e in range(2):
                        T = 2 * t + e
                        dve.wait_ge(*((chunk_used, 2 * t + 2) if e else (tile_done, t + 1)))
                        dst = ckv[:, t, e * SEQ:(e + 1) * SEQ] if t < 4 else kro[:, e * SEQ:(e + 1) * SEQ]
                        dve.tensor_copy(dst, bank[T % 4][:, 0:SEQ]).then_inc(tile_taken, 1)
                else:
                    T = 10 + t - 5
                    dve.wait_ge(chunk_used, 2 * t + 2)
                    dve.tensor_copy(cq[:, t - 5, :], bank[T % 4][:, 0:SEQ]).then_inc(tile_taken, 1)
                if t == 0:
                    dve.wait_ge(acc_zeroed, 1)
                for _ in range((5, 4, 2)[(t > 3) + (t > 4)]):
                    ada_step(0, a // 2, a % 4, a)
                    a += 1
                for c in (2 * t + 4, 2 * t + 5):
                    split(c, c % RING)
                if t == 4:
                    dve.wait_ge(norm_summed, NRM_KV + 1)
                    dve.tensor_scalar(rstd[:, :], bank[6][:, :], 1.0 / LORA, EPS, ALU.mult, ALU.add)\
                        .then_inc(var_done, 1)
                    invert(2, NTOK)
                    for m in range(LT):
                        dve.scalar_tensor_tensor(ckv[:, m, :], ckv[:, m, :], lgain_s[:, 1, m:m + 1], rstd[:, :],
                                                 ALU.mult, ALU.mult).then_inc(lat_pre, 1)
                if t == 5:
                    for m in range(LT):
                        dve.wait_ge(lat_hi, m + 1)
                        lo_of(ckv_lo[:, m, :], ckv[:, m, :], ckv_hi[:, m, :], lat_ready)
                    dve.wait_ge(kr_rot, 1)
                    dve.tensor_tensor(krt[:, :], bank[7][:, 0:SEQ], sin, ALU.mult).then_inc(kr_step, 1)
                    dve.tensor_tensor(kro[:, SEQ:NTOK], kro[:, SEQ:NTOK], cos, ALU.mult).then_inc(kr_step, 1)
                    dve.wait_ge(kr_step, 2)
                    dve.tensor_tensor(kro[:, SEQ:NTOK], kro[:, SEQ:NTOK], krt[:, :], ALU.add).then_inc(kr_step, 1)
                    dve.memset(kr_hi[ROPE:P, 0, :].bitcast(f32), 0.0).then_inc(kr_zero, 1)
                    dve.memset(kr_lo[ROPE:P, 0, :].bitcast(f32), 0.0).then_inc(kr_zero, 1)
                    dve.memset(kr_hi[0:ROPE, 1, :].bitcast(f32), 0.0).then_inc(kr_zero, 1)
                    dve.memset(kr_lo[0:ROPE, 1, :].bitcast(f32), 0.0).then_inc(kr_zero, 1)
                if t == 6:
                    dve.wait_ge(kr_hi_done, 1)
                    lo_of(kr_lo[0:ROPE, 0, :], kro[0:ROPE, :], kr_hi[0:ROPE, 0, :], kr_ready)
                    dve.wait_ge(kr_hi_done, 2)
                    lo_of(kr_lo[ROPE:P, 1, :], kro[ROPE:P, :], kr_hi[ROPE:P, 1, :], kr_ready)
            dve.wait_ge(norm_summed, NRM_Q + 1)
            dve.tensor_scalar(rstd[:, 0:SEQ], bank[6][:, 0:SEQ], 1.0 / LORA, EPS, ALU.mult, ALU.add)\
                .then_inc(var_done, 1)
            invert(3, SEQ)
            for m in range(LT):
                dve.scalar_tensor_tensor(cq[:, m, :], cq[:, m, :], lgain_s[:, 0, m:m + 1], rstd[:, 0:SEQ],
                                         ALU.mult, ALU.mult).then_inc(lat_pre, 1)
            for m in range(LT):
                dve.wait_ge(lat_hi, LT + m + 1)
                lo_of(cq_lo[:, m, :], cq[:, m, :], cq_hi[:, m, :], lat_ready)
            mods(0)

            def v_lo_parts(v_count, buf, q):
                for e in range(2):
                    dve.wait_ge(v_hi_done, v_count + e + 1)
                    lo_of(v_lo[:, buf, 2 * e:2 * e + 2, :], bank[e][:, :].rearrange("p (t n) -> p t n", t=2),
                          v_hi[:, buf, 2 * e:2 * e + 2, :], proj_taken)

            def kq_lo_parts(n, buf):
                dve.wait_ge(kq_hi, 2 * n + 1)
                lo_of(kn_lo[:, buf, :], bank[0][:, :], kn_hi[:, buf, :], proj_taken)
                dve.wait_ge(kq_hi, 2 * n + 2)
                lo_of(qn_lo[:, buf, :], bank[1][:, 0:SEQ], qn_hi[:, buf, :], proj_taken)

            def rope_take(c):
                dve.wait_ge(chunk_used, c + 1)
                dve.tensor_copy(qraw[:, :], bank[0][:, 0:SEQ]).then_inc(proj_taken, 1)

            def rope_turn(p, q, n_proj):
                dve.wait_ge(proj_taken, q + 1)
                dve.tensor_tensor(tq[:, :], qraw[:, :], cos, ALU.mult).then_inc(rope_step, 1)
                dve.wait_ge(proj_done, n_proj)
                dve.wait_ge(rope_step, 3 * p + 1)
                dve.tensor_tensor(qraw[:, :], bank[1][:, 0:SEQ], sin, ALU.mult).then_inc(proj_taken, 1)
                dve.wait_ge(proj_taken, q + 2)
                dve.tensor_tensor(tq[:, :], tq[:, :], qraw[:, :], ALU.add).then_inc(rope_step, 2)

            def rope_lo(p, buf):
                dve.wait_ge(qr_hi_done, p + 1)
                lo_of(qr_lo[:, buf, :], tq[:, :], qr_hi[:, buf, :], qr_ready)

            v_lo_parts(0, 0, 0)
            split(22, 22 % RING)
            kq_lo_parts(0, 0)
            rope_take(C_HEAD + 2)
            rope_turn(0, 4, 3)
            split(23, 23 % RING)
            rope_lo(0, 0)
            split(24, 24 % RING)
            dve.wait_ge(acc_zeroed, ADA_ACCS[1] + 1)

            def step(n, s, p, last, top):
                for qt in range(2):
                    dve.wait_ge(s_done, 2 * n + qt + 1)
                    dve.reduce_max(mx[:, qt:qt + 1], bank[4 + qt][:, :], axis=AX.X).then_inc(mx_done, 1)
                    dve.wait_ge(mx_done, 2 * n + qt + 1)
                    dve.tensor_scalar(negmax[:, qt:qt + 1], mx[:, qt:qt + 1], -SM_SCALE, None, ALU.mult)\
                        .then_inc(negmax_done, 1)
                q = proj_index(n)
                if last < 1:
                    kq_lo_parts(n + 1, (s + 1) % 2)
                if s % 2 and last < 0:
                    rope_take(head_chunk(n) + 1)
                dve.wait_ge(exp_done, 2 * n + 2)
                dve.reciprocal(rinv[:, :], psum_row[:, :]).then_inc(rinv_done, 1)
                dve.wait_ge(rinv_done, n + 1)
                for qt in range(2):
                    dve.tensor_scalar(diag[:, qt, :], ident, rinv[:, qt:qt + 1], None, ALU.mult).then_inc(diag_done, 1)
                for e in range(2):
                    ada_step(1, n, 2 * s + e, ADA_AT[1] + 2 * n + e)
                for qt in range(2):
                    dve.wait_ge(pt_hi_done, 2 * n + qt + 1)
                    lo_of(pt_lo[:, :, qt * P:(qt + 1) * P], bank[6 + qt][:, :].rearrange("p (t n) -> p t n", t=4),
                          pt_hi[:, :, qt * P:(qt + 1) * P], pt_ready)
                c = C_HEAD + 7 + 2 * n
                if s % 2 == 0:
                    if last < 0:
                        v_lo_parts(n + 2, (s // 2 + 1) % 2, q + 2)
                    if top is None or c <= top:
                        split(c, (C_HEAD + 7 + 2 * s) % RING)
                else:
                    if last < 0:
                        rope_turn(p, q + 2, proj_at(n) + 2)
                    if top is None or c <= top:
                        split(c, (C_HEAD + 7 + 2 * s) % RING)
                    if last < 0:
                        rope_lo(p, (s // 2 + 1) % 2)
                if top is None or c + 1 <= top:
                    split(c + 1, (C_HEAD + 8 + 2 * s) % RING)
                dve.wait_ge(o_hi_done, n + 1)
                lo_of(row(h_lo, n), bank[3][:, 0:SEQ], row(h_hi, n), o_ready)

            with dve.Fori(0, 3) as i:
                for s in range(4):
                    step(4 * i + s, s, 2 * i + (s + 1) // 2, -1, None)
            for s in range(4):
                step(12 + s, s, 6 + (s + 1) // 2, (s > 1) + (s > 2) - 1, C_WO + 3)
            mods(1)
            scales(2, mod[:, SC2, :], 2, MODS_EARLY + 2)
            dve.wait_ge(acc_zeroed, ADA_ACCS[2] + 1)

            def residual(m, e, gate, *after):
                dve.wait_ge(*after)
                xm = row(x, m)
                g = one(mod[:, gate:gate + 1, bass.ds(m, 1)])
                dve.scalar_tensor_tensor(xm, bank[4 + e][:, 0:SEQ], g, xm, ALU.mult, ALU.add).then_inc(y_free, 1)

            def square(c0, b, gate, loops, limit):
                for c in (c0 + 4, c0 + 5, c0 + 6):
                    split(c, c % RING)

                def body(i, top):
                    for t in range(2):
                        residual(2 * i + t, t, gate, chunk_used, c0 + 4 * i + 2 * t + 2)
                        for e in range(2):
                            ada_step(b, 2 * i + t, 2 * t + e, ADA_AT[b] + 4 * i + 2 * t + e)
                        for e in range(2):
                            c = c0 + 4 * i + 7 + 2 * t + e
                            if top is None or c <= top:
                                split(c, (c0 + 7 + 2 * t + e) % RING)

                with dve.Fori(0, loops) as i:
                    body(i, None)
                body(loops, limit)

            def norm(k, n_sum):
                dve.wait_ge(norm_summed, n_sum + 1)
                dve.tensor_scalar(rstd[:, 0:SEQ], bank[6][:, 0:SEQ], 1.0 / D, EPS, ALU.mult, ALU.add)\
                    .then_inc(var_done, 1)
                invert(k, SEQ)

            def normed(k, n_sum, h0, i, shift):
                norm(k, n_sum)
                for m in range(KT + 2):
                    if m < KT:
                        dve.scalar_tensor_tensor(h_pre[:, m, :], x[:, m, :], scl[:, i, m:m + 1], rstd[:, 0:SEQ],
                                                 ALU.mult, ALU.mult).then_inc(pre_done, 1)
                    if m >= 2:
                        j = m - 2
                        dve.wait_ge(h_hi_done, h0 + j + 1)
                        dve.scalar_tensor_tensor(h_lo[:, j, :], h_pre[:, j, :], mod[:, shift, j:j + 1],
                                                 h_hi[:, j, :].bitcast(f32), ALU.add, ALU.subtract).then_inc(h_ready, 1)

            def ffn(c0, T0, P0, layer):
                for c in (c0 + 4, c0 + 5, c0 + 6):
                    split(c, c % RING)
                dve.wait_ge(conv_in, 16 * (layer + 1))

                def pair(c, T, Pn, f, j, s, ada_ops):
                    split(c + 7, (c0 + 7) % RING)
                    taps = [conv_s[:, bass.ds(2 * f + g, 1), :] for g in range(2)]
                    banks = [bank[(T0 + 2 * s + g) % 4] for g in range(2)]
                    for g in range(2):
                        dve.wait_ge(mid_done, 2 * Pn + g + 1)
                        dve.scalar_tensor_tensor(cv[:, s, g, 1:SEQ], banks[g][:, 0:SEQ - 1], taps[g][:, :, 0],
                                                 cv[:, s, g, 1:SEQ], ALU.mult, ALU.add).then_inc(left_done, 1)
                    for g in range(2):
                        dve.wait_ge(left_done, 2 * Pn + g + 1)
                        dve.scalar_tensor_tensor(cv[:, s, g, 0:SEQ - 1], banks[g][:, 1:SEQ], taps[g][:, :, 2],
                                                 cv[:, s, g, 0:SEQ - 1], ALU.mult, ALU.add).then_inc(tile_taken, 1)
                    ada_ops()
                    split(c + 8, (c0 + 8) % RING)
                    dve.wait_ge(silu_done, Pn + 1)
                    dve.tensor_tensor(ga[:, :], cv[:, s, 0, :], cv[:, s, 1, :], ALU.mult).then_inc(gated, 1)
                    dve.wait_ge(a_hi_done, Pn + 1)
                    lo_of(row(a_lo, j), ga[:, :], row(a_hi, j), a_ready)
                    split(c + 9, (c0 + 9) % RING)
                    split(c + 10, (c0 + 10) % RING)

                def up(i, ada_ops):
                    for s in range(2):
                        j = 2 * i + s
                        pair(c0 + 8 * i + 4 * s, T0 + 4 * i + 2 * s, P0 + j, j, j, s, lambda: ada_ops(i, s))

                def both(i, s):
                    for e in range(2):
                        ada_step(3, i, 2 * s + e, ADA_AT[3] + 4 * i + 2 * s + e)

                def single(i, s):
                    for e in range(2):
                        ada_step(7, 2 * i + s, 2 * s + e, ADA_AT[7] + 4 * i + 2 * s + e)

                if layer == 0:
                    dve.wait_ge(acc_zeroed, ADA_ACCS[3] + 2)
                    with dve.Fori(0, 16) as i:
                        up(i, both)
                    mods(3)
                    dve.wait_ge(acc_zeroed, ADA_ACCS[4] + 2)
                else:
                    dve.wait_ge(acc_zeroed, ADA_ACCS[7] + 1)
                    with dve.Fori(0, 8) as i:
                        up(i, single)
                    with dve.Fori(8, 16) as i:
                        up(i, lambda i, s: None)
                    mods(7)
                gate = 6 * layer + G2
                dve.wait_ge(mod_done, MOD_G2[layer])
                c1 = c0 + 4 * PARTS[0]
                with dve.Fori(0, KT // 2) as i:
                    for t in range(2):
                        m = 2 * i + t
                        residual(m, t, gate, chunk_used, c1 + 4 * m + 4)
                        split(c1 + 4 * m + 7, (c1 + 7) % RING)
                        if layer == 0:
                            for e in range(4):
                                ada_step(4, m, e, ADA_AT[4] + 4 * m + e)
                        for e in range(1, 4):
                            split(c1 + 4 * m + 7 + e, (c1 + 7 + e) % RING)
                if layer == 0:
                    mods(4)
                    scales(3, mod[:, 6 + SC1, :], 1, MODS_EARLY + 5)
                c2 = c1 + 2 * PARTS[0]
                with dve.Fori(0, PARTS[1] // 2) as i:
                    for s in range(2):
                        j = 2 * i + s
                        pair(c2 + 8 * i + 4 * s, T0 + 2 * PARTS[0] + 4 * i + 2 * s, P0 + PARTS[0] + j,
                             PARTS[0] + j, j, s, lambda: None)
                c3 = c2 + 4 * PARTS[1]
                for t in range(8):
                    for e in range(2):
                        residual(2 * t + e, e, gate,
                                 *((chunk_used, c3 + 3 * t + 3) if e else (y_done, 8 * layer + t + 1)))
                    for c in range(c3 + 3 * t + 7, c3 + 3 * t + 10):
                        if c <= min(c3 + 24 + 3, N_CHUNKS - 1):
                            split(c, c % RING)

            dve.wait_ge(mod_done, MODS_EARLY + 1)
            square(C_WO, 2, G1, 7, C_FFN0 + 3)
            mods(2)
            dve.wait_ge(scl_done, 3)
            normed(4, NRM_L0F, H_L0F, 2, SH2)
            ffn(C_FFN0, T_UP0, 0, 0)
            dve.wait_ge(dft_hi_done, 1)
            lo_of(dft_lo[:, :, :], dft_s[:, :, :], dft_hi[:, :, :], dft_ready)
            dve.wait_ge(scl_done, 4)
            normed(5, NRM_L1, H_L1, 3, 6 + SH1)
            dve.wait_ge(acc_zeroed, ADA_ACCS[5] + 1)

            def spectrum(g):
                for t in range(2):
                    dve.wait_ge(ab_hi_done, 2 * g + t + 1)
                    lo_of(ab_lo[:, g % 2, t, :], bank[4 + t][:, :], ab_hi[:, g % 2, t, :], ab_ready)

            def back(g):
                for m in (2 * g, 2 * g + 1):
                    dve.wait_ge(f_hi_done, m + 1)
                    lo_of(f_lo[:, m, :], bank[(T_DFT + m) % 4][:, 0:SEQ], f_hi[:, m, :], tile_taken)

            for g in range(9):
                if g < 8:
                    spectrum(g)
                    for e in range(4):
                        ada_step(5, 2 * g + e // 2, e, ADA_AT[5] + 4 * g + e)
                if g:
                    back(g - 1)
            mods(5)
            dve.wait_ge(acc_zeroed, ADA_ACCS[6] + 1)
            square(C_FNO, 6, 6 + G1, 7, C_FFN1 + 3)
            mods(6)
            scales(4, mod[:, 6 + SC2, :], 3, MODS_EARLY + 7)
            dve.wait_ge(scl_done, 5)
            normed(6, NRM_L1F, H_L1F, 4, 6 + SH2)
            ffn(C_FFN1, T_UP1, FT, 1)
            norm(7, NRM_OUT)
            for m in range(KT):
                dve.scalar_tensor_tensor(h_pre[:, m, :], x[:, m, :], gain_s[:, 4, m:m + 1], rstd[:, 0:SEQ],
                                         ALU.mult, ALU.mult).then_inc(pre_done, 1)

        @block.tensor
        def _(pe):
            def product(out, slot, u, hi_part, lo_part, first, last):
                wh = w_hi[:, slot, u * UNIT:(u + 1) * UNIT]
                wl = w_lo[:, slot, u * UNIT:(u + 1) * UNIT]
                pe.matmul(out, wh, hi_part, start=first, stop=False)
                pe.matmul(out, wh, lo_part, start=False, stop=False)
                return pe.matmul(out, wl, hi_part, start=False, stop=last)

            def moving(out, a_h, a_l, b_h, b_l, first, last):
                pe.matmul(out, a_h, b_h, start=first, stop=False)
                pe.matmul(out, a_h, b_l, start=False, stop=False)
                return pe.matmul(out, a_l, b_h, start=False, stop=last)

            def norm_sum(cols, need):
                pe.wait_ge(sq_done, need)
                pe.matmul(bank[6][:, 0:cols], ones, sq[:, 0:cols], start=True, stop=True)\
                    .then_inc(norm_summed, 1)

            def ada_sum(b):
                pe.wait_ge(ada_used, ADA_AT[b + 1])
                for n in range(ADA_BLOCKS[b][1]):
                    acc = (acc0, acc1)[n]
                    for j in range(KT):
                        mm = pe.matmul(bank[7][:, n * KT + j:n * KT + j + 1], acc[:, j * P:(j + 1) * P],
                                       ones[:, 0:1], start=True, stop=True)
                mm.then_inc(ada_summed, 1)

            pe.wait_ge(small_in, 16 * 5)
            for n, src in enumerate((ctx_sq, h_pre)):
                pe.wait_ge(sq0_done, n + 1)
                for k in range(KT):
                    mm = pe.matmul(bank[6][:, n * SEQ:(n + 1) * SEQ], ones, src[:, k, :],
                                   start=(k == 0), stop=(k == KT - 1))
                mm.then_inc(norm_summed, 1)
            pe.wait_ge(silu_c_done, 1)
            with pe.Fori(0, N_EARLY // RING) as i:
                for s in range(RING):
                    pe.wait_ge(ada_in[s], 16 * (i + 1))
                    for u in range(8):
                        k = (s % 2) * 8 + u
                        mm = pe.matmul(bank[0][:, bass.ds(4 * i + 2 * (s // 2), 2)],
                                       ada[:, s, u * UNIT:(u + 1) * UNIT], silu_c[:, k, :],
                                       start=(k == 0), stop=(k == KT - 1))
                    mm.then_inc(ada_used_pe, 1)

            for t in range(9):
                for e in range(2 if t < 5 else 1):
                    T = 2 * t + e if t < 5 else 10 + t - 5
                    context = t < 5 and e == 0
                    hh, hl, h0 = (hc_hi, hc_lo, 0) if context else (h_hi, h_lo, KT)
                    if T >= 4:
                        pe.wait_ge(tile_taken, T - 3)
                    elif T == 0:
                        pe.wait_ge(mod_done, MODS_EARLY)
                    for k in range(KT):
                        c = 2 * t + k // 8
                        if k % 8 == 0:
                            pe.wait_ge(lo_done, c + 1)
                        if t == 0:
                            pe.wait_ge(h_ready, h0 + k + 1)
                        mm = product(bank[T % 4][:, 0:SEQ], c % RING, k % 8, hh[:, k, :], hl[:, k, :],
                                     k == 0, k == KT - 1)
                        if not context and k % 8 == 7:
                            mm.then_inc(chunk_used, 1)
                    if context:
                        mm.then_inc(tile_done, 1)
                if t == 5:
                    norm_sum(NTOK, 8)
                if t == 6:
                    pe.wait_ge(tile_taken, 10)
                    pe.matmul(bank[7][:, 0:SEQ], rot, kro[:, SEQ:NTOK], start=True, stop=True).then_inc(kr_rot, 1)

            def values(buf, slot, c, q):
                pe.wait_ge(lo_done, c + 1)
                for e in range(2):
                    pe.wait_ge(proj_taken, q + e - 1)
                    for t in range(2):
                        tok = slice((2 * e + t) * P, (2 * e + t + 1) * P)
                        for k in range(LT):
                            w = slice(2 * k * UNIT, 2 * (k + 1) * UNIT)
                            mm = moving(bank[e][:, t * 2 * VD:(t + 1) * 2 * VD], ckv_hi[:, k, tok], ckv_lo[:, k, tok],
                                        w_hi[:, slot, w], w_lo[:, slot, w], k == 0, k == LT - 1)
                    mm.then_inc(chunk_used if e else proj_done, 1)

            def keys_queries(slot, c, q):
                pe.wait_ge(lo_done, c + 1)
                pe.wait_ge(proj_taken, q - 1)
                for k in range(LT):
                    mm = product(bank[0][:, :], slot, k, ckv_hi[:, k, :], ckv_lo[:, k, :], k == 0, k == LT - 1)
                mm.then_inc(proj_done, 1)
                pe.wait_ge(proj_taken, q)
                for k in range(LT):
                    mm = product(bank[1][:, 0:SEQ], slot, 4 + k, cq_hi[:, k, :], cq_lo[:, k, :], k == 0, k == LT - 1)
                mm.then_inc(chunk_used, 1)

            def rope_queries(slot, c, q):
                pe.wait_ge(lo_done, c + 1)
                pe.wait_ge(proj_taken, q - 1)
                for k in range(LT):
                    mm = product(bank[0][:, 0:SEQ], slot, k, cq_hi[:, k, :], cq_lo[:, k, :], k == 0, k == LT - 1)
                mm.then_inc(chunk_used, 1)

            def rotate(q):
                pe.wait_ge(proj_taken, q + 1)
                pe.matmul(bank[1][:, 0:SEQ], rot, qraw[:, :], start=True, stop=True).then_inc(proj_done, 1)

            pe.wait_ge(tile_taken, 14)
            norm_sum(SEQ, SQ_LAT)
            pe.wait_ge(lat_ready, LT)
            pe.wait_ge(lo_done, C_HEAD + 1)
            for e in range(2):
                for t in range(2):
                    tok = slice((2 * e + t) * P, (2 * e + t + 1) * P)
                    for k in range(LT):
                        w = slice(2 * k * UNIT, 2 * (k + 1) * UNIT)
                        mm = moving(bank[e][:, t * 2 * VD:(t + 1) * 2 * VD], ckv_hi[:, k, tok], ckv_lo[:, k, tok],
                                    w_hi[:, C_HEAD % RING, w], w_lo[:, C_HEAD % RING, w], k == 0, k == LT - 1)
                mm.then_inc(chunk_used if e else proj_done, 1)
            ada_sum(0)
            pe.wait_ge(lat_ready, 2 * LT)
            keys_queries((C_HEAD + 1) % RING, C_HEAD + 1, 2)
            rope_queries((C_HEAD + 2) % RING, C_HEAD + 2, 4)
            rotate(4)
            pe.wait_ge(kr_ready, 2)
            pe.wait_ge(kr_zero, 4)

            def step(n, s, p, last):
                buf, pair = s % 2, (s // 2) % 2
                q, c = proj_index(n), head_chunk(n)
                slots = [(C_HEAD + 3 + 2 * s + e) % RING for e in range(2)]
                pe.wait_ge(proj_taken, 4 * n + 4)
                pe.wait_ge(qr_ready, p if s % 2 else p + 1)
                for qt in range(2):
                    rows = slice(qt * P, (qt + 1) * P)
                    out = bank[4 + qt][:, :]
                    moving(out, qn_hi[:, buf, rows], qn_lo[:, buf, rows], kn_hi[:, buf, :], kn_lo[:, buf, :], True, False)
                    moving(out, qr_hi[:, pair, rows], qr_lo[:, pair, rows], kr_hi[:, buf, :], kr_lo[:, buf, :],
                           False, True).then_inc(s_done, 1)
                if last < 1:
                    keys_queries(slots[0], c, q)
                if s % 2 and last < 0:
                    rope_queries(slots[1], c + 1, q + 2)
                for qt in range(2):
                    pe.wait_ge(diag_done, 2 * n + qt + 1)
                    for t in range(4):
                        mm = pe.matmul(bank[6 + qt][:, t * P:(t + 1) * P], prob[:, qt, t * P:(t + 1) * P],
                                       diag[:, qt, :], start=True, stop=True)
                    mm.then_inc(t_done, 1)
                if last < 0:
                    if s % 2:
                        rotate(q + 2)
                    else:
                        values((s // 2 + 1) % 2, slots[1], c + 1, q + 2)
                pe.wait_ge(pt_ready, 2 * n + 2)
                pe.wait_ge(o_ready, n)
                v = slice(buf * VD, (buf + 1) * VD)
                for t in range(4):
                    mm = moving(bank[3][:, 0:SEQ], v_hi[:, pair, t, v], v_lo[:, pair, t, v], pt_hi[:, t, :],
                                pt_lo[:, t, :], t == 0, t == 3)
                mm.then_inc(o_done, 1)

            with pe.Fori(0, 3) as i:
                for s in range(4):
                    step(4 * i + s, s, 2 * i + (s + 1) // 2, -1)
            for s in range(4):
                step(12 + s, s, 6 + (s + 1) // 2, (s > 1) + (s > 2) - 1)
            ada_sum(1)

            def square(c0, Y0, hh, hl):
                with pe.Fori(0, KT // 2) as i:
                    for t in range(2):
                        pe.wait_ge(y_free, Y0 + 2 * i + t + 1)
                        for k in range(KT):
                            e = 2 * t + k // 8
                            if k % 8 == 0:
                                pe.wait_ge(lo_done, c0 + 4 * i + e + 1)
                            mm = product(bank[4 + t][:, 0:SEQ], (c0 + e) % RING, k % 8, hh[:, k, :], hl[:, k, :],
                                         k == 0, k == KT - 1)
                            if k % 8 == 7:
                                mm.then_inc(chunk_used, 1)

            def up(c0, T0, i, h0):
                for g in range(4):
                    pe.wait_ge(tile_taken, T0 + 4 * i + g - 3)
                    for k in range(KT):
                        e = 2 * g + k // 8
                        if k % 8 == 0:
                            pe.wait_ge(lo_done, c0 + 8 * i + e + 1)
                        if g == 0 and h0 is not None:
                            pe.wait_ge(h_ready, h0 + k + 1)
                        mm = product(bank[(T0 + g) % 4][:, 0:SEQ], (c0 + e) % RING, k % 8, h_hi[:, k, :],
                                     h_lo[:, k, :], k == 0, k == KT - 1)
                        if k % 8 == 7:
                            mm.then_inc(chunk_used, 1)

            def ffn(c0, T0, P0, Y0, h0, layer):
                with pe.Fori(0, PARTS[0] // 2) as i:
                    up(c0, T0, i, h0)
                ada_sum(3 if layer == 0 else 7)
                c1 = c0 + 4 * PARTS[0]
                with pe.Fori(0, KT // 2) as i:
                    for t in range(2):
                        pe.wait_ge(y_free, Y0 + 2 * i + t + 1)
                        for k in range(PARTS[0]):
                            e = 4 * t + k // 8
                            if k % 8 == 0:
                                pe.wait_ge(lo_done, c1 + 8 * i + e + 1)
                                pe.wait_ge(a_ready, P0 + k + 8)
                            mm = product(bank[4 + t][:, 0:SEQ], (c1 + e) % RING, k % 8, a_hi[:, k, :], a_lo[:, k, :],
                                         k == 0, k == PARTS[0] - 1)
                            if k % 8 == 7:
                                mm.then_inc(chunk_used, 1)
                if layer == 0:
                    ada_sum(4)
                c2 = c1 + 2 * PARTS[0]
                with pe.Fori(0, PARTS[1] // 2) as i:
                    up(c2, T0 + 2 * PARTS[0], i, None)
                c3 = c2 + 4 * PARTS[1]
                for t in range(KT):
                    pe.wait_ge(y_free, Y0 + KT + t + 1)
                    for k in range(PARTS[1]):
                        u = PARTS[1] * t + k
                        c = c3 + u // 8
                        if u % 8 == 0:
                            pe.wait_ge(lo_done, c + 1)
                        if t == 0:
                            pe.wait_ge(a_ready, P0 + PARTS[0] + k + 1)
                        mm = product(bank[4 + t % 2][:, 0:SEQ], c % RING, u % 8, a_hi[:, k, :], a_lo[:, k, :],
                                     k == 0, k == PARTS[1] - 1)
                        if u % 8 == 7:
                            mm.then_inc(chunk_used, 1)
                    if t % 2 == 0:
                        mm.then_inc(y_done, 1)

            pe.wait_ge(o_ready, HEADS)
            square(C_WO, Y_WO, h_hi, h_lo)
            ada_sum(2)
            norm_sum(SEQ, SQ_LAT + SQ_ADDS)
            ffn(C_FFN0, T_UP0, 0, Y_FFN0, H_L0F, 0)
            norm_sum(SEQ, SQ_LAT + 2 * SQ_ADDS)

            def spectrum(g):
                for t in range(2):
                    if g:
                        pe.wait_ge(ab_ready, 2 * g - 1 + t)
                    for k in range(2):
                        tok = slice(t * P, (t + 1) * P)
                        m = 2 * g + k
                        pe.wait_ge(h_ready, H_L1 + m + 1)
                        mm = moving(bank[4 + t][:, :], h_hi[:, m, tok], h_lo[:, m, tok], dft_hi[:, k, 0:2 * SEQ],
                                    dft_lo[:, k, 0:2 * SEQ], k == 0, k == 1)
                    mm.then_inc(ab_done, 1)

            def back(g):
                for m in range(2):
                    T = T_DFT + 2 * g + m
                    pe.wait_ge(tile_taken, T - 3)
                    pe.wait_ge(ab_ready, 2 * g + 2)
                    for n, (t, part, table) in enumerate(((0, 0, 0), (1, 0, 0), (0, SEQ, 2 * SEQ), (1, SEQ, 2 * SEQ))):
                        ch = slice(part + m * P, part + (m + 1) * P)
                        to = slice(table, table + SEQ)
                        mm = moving(bank[T % 4][:, 0:SEQ], ab_hi[:, g % 2, t, ch], ab_lo[:, g % 2, t, ch],
                                    dft_hi[:, t, to], dft_lo[:, t, to], n == 0, n == 3)
                    mm.then_inc(tile_done, 1)

            pe.wait_ge(dft_ready, 1)
            for g in range(9):
                if g < 8:
                    spectrum(g)
                if g:
                    back(g - 1)
            ada_sum(5)
            pe.wait_ge(tile_taken, T_UP1)
            square(C_FNO, Y_FNO, f_hi, f_lo)
            ada_sum(6)
            norm_sum(SEQ, SQ_LAT + 3 * SQ_ADDS)
            ffn(C_FFN1, T_UP1, FT, Y_FFN1, H_L1F, 1)
            norm_sum(SEQ, SQ_LAT + 4 * SQ_ADDS)


def tile_blocks(w, order=None):
    k, m = w.shape
    return w.reshape(k // P, P, m // P, P).transpose(2, 0, 1, 3)


def as_chunks(blocks):
    return blocks.reshape(-1, 8, P, P).transpose(0, 2, 1, 3).reshape(-1, P, CH)


def weight_stream(w_dqkv, w_uq, w_ukv, w_o, fno_w, w_up, w_down):
    out = np.empty((N_CHUNKS, P, CH), np.float32)
    at = [0]

    def put(chunks):
        out[at[0]:at[0] + len(chunks)] = chunks
        at[0] += len(chunks)

    put(as_chunks(tile_blocks(w_dqkv[:, LORA:2 * LORA])))
    kr = w_dqkv[:, 2 * LORA:]
    put(as_chunks(tile_blocks(np.concatenate([kr, kr], 1))))
    put(as_chunks(tile_blocks(w_dqkv[:, :LORA])))
    q = w_uq.reshape(LORA, HEADS, P + ROPE)
    kv = w_ukv.reshape(LORA, HEADS, P + VD)

    def kq(h):
        return as_chunks(np.concatenate([tile_blocks(kv[:, h, :P])[0], tile_blocks(q[:, h, :P])[0]]))

    def values(p):
        w = kv[:, 2 * p:2 * p + 2, P:].reshape(LT, P, 2 * VD)
        return w.transpose(1, 0, 2).reshape(1, P, CH)

    def rope_q(p):
        w = np.zeros((8, P, P), np.float32)
        w[:LT] = tile_blocks(q[:, 2 * p:2 * p + 2, P:].reshape(LORA, P))[0]
        return as_chunks(w)

    put(values(0))
    put(kq(0))
    put(rope_q(0))
    for n in range(HEADS - 1):
        put(kq(n + 1))
        if n < HEADS - 2:
            put(rope_q(n // 2 + 1) if n % 2 else values(n // 2 + 1))
    put(as_chunks(tile_blocks(w_o)))
    for layer in range(2):
        if layer:
            put(as_chunks(tile_blocks(fno_w)))
        up = tile_blocks(w_up[layer])
        up = np.stack([up[:FT], up[FT:]], 1)
        down = tile_blocks(w_down[layer])
        lo = 0
        for n in PARTS:
            put(as_chunks(up[lo:lo + n]))
            put(as_chunks(down[:, lo:lo + n]))
            lo += n
    assert at[0] == N_CHUNKS
    return out


def constants():
    ident_ones = np.stack([np.eye(P), np.ones((P, P))], 1).astype(np.float32)
    half = ROPE // 2
    inv = np.power(np.float32(10000.0), -np.arange(0, half, 2, dtype=np.float32) / np.float32(half))
    pos = np.arange(SEQ)
    ang_r = (pos // GRID_W).astype(np.float32)[:, None] * inv
    ang_c = (pos % GRID_W).astype(np.float32)[:, None] * inv
    ang = np.concatenate([ang_r, ang_r, ang_c, ang_c], -1).T
    ang = np.concatenate([ang, ang], 0)
    turn = np.zeros((P, P), np.float32)
    for b in range(0, P, half):
        for j in range(half // 2):
            turn[b + half // 2 + j, b + j] = -1.0
            turn[b + j, b + half // 2 + j] = 1.0
    rope = np.concatenate([np.cos(ang), np.sin(ang), turn], 1).astype(np.float32)
    nk = np.outer(np.arange(SEQ), np.arange(SEQ)) % SEQ
    c, s = np.cos(2 * np.pi * nk / SEQ) / 16, np.sin(2 * np.pi * nk / SEQ) / 16
    dft = np.concatenate([c, s, -s], 1).reshape(2, P, 3 * SEQ).transpose(1, 0, 2).astype(np.float32)
    return ident_ones, rope, dft


def kernel(**inputs):
    import numpy as _np
    import concourse.bacc as _bacc
    from concourse import mybir as _mybir
    from concourse.bass_utils import run_bass_kernel_spmd as _run

    g = {k: _np.asarray(v) for k, v in inputs.items()}

    def columns(v):
        return _np.moveaxis(v.reshape(v.shape[:-1] + (-1, P)), -1, 0)

    ident_ones, rope, dft = constants()
    aw = g["ada_w"].reshape(2, D, 6, D)
    early = _np.concatenate([as_chunks(tile_blocks(aw[0, :, m])) for m in (SH1, SC1)])
    rows = aw.reshape(2, KT, P, 6, 2, CH).transpose(0, 3, 1, 4, 2, 5).reshape(12, KT, 2, P, CH)
    late = _np.empty((N_ADA, P, CH), _np.float32)
    for b, (first, n) in enumerate(ADA_BLOCKS):
        late[ADA_AT[b]:ADA_AT[b + 1]] = rows[first:first + n].transpose(1, 0, 2, 3, 4).reshape(-1, P, CH)
    conv = _np.concatenate([g["ffn_conv_w"], g["ffn_conv_b"][:, None]], 1)
    conv = conv.reshape(2, 4, 2, FT, P).transpose(0, 4, 3, 2, 1).reshape(2, P, 2 * FT, 4)
    arrays = {
        "xT": columns(g["x"][0]).transpose(0, 2, 1),
        "ctxT": columns(g["ctx"][0]).transpose(0, 2, 1),
        "cond": columns(_np.stack([g["c"][0], g["c_ctx"]])).transpose(0, 2, 1),
        "ada_early": early,
        "ada_late": late,
        "ada_b": columns(g["ada_b"].reshape(12, D)),
        "gains": columns(_np.concatenate([g["norm1_g"], g["norm2_g"], g["final_norm_g"][None]])),
        "lat_gains": columns(_np.concatenate([g["mla_q_norm_g"], g["mla_kv_norm_g"]])),
        "weights": weight_stream(g["mla_w_dqkv"][0], g["mla_w_uq"][0], g["mla_w_ukv"][0], g["mla_w_o"][0],
                                 g["fno_w"][0], g["ffn_w_up"], g["ffn_w_down"]),
        "conv": conv,
        "consts": ident_ones,
        "rope": rope,
        "dft": dft,
    }
    nc = _bacc.Bacc("TRN2", target_bir_lowering=False, num_devices=1)
    args = []
    for name, a in arrays.items():
        arrays[name] = a = _np.ascontiguousarray(a)
        args.append(nc.dram_tensor(name, a.shape, _mybir.dt.from_np(a.dtype), kind="ExternalInput").ap())
    out = nc.dram_tensor("outT", (P, KT, SEQ), _mybir.dt.float32, kind="ExternalOutput").ap()
    backbone(nc, *args, out)
    r = _run(nc, [arrays], core_ids=[0])
    got = r.results[0]["outT"]
    return _np.ascontiguousarray(got.transpose(2, 1, 0)).reshape(1, SEQ, D)
```

```python
from contextlib import ExitStack

import numpy as np
import concourse.bass as bass
from concourse import mybir

P = 128
D = 2048
KT = D // P
SEQ = 256
NTOK = 2 * SEQ
HEADS = 16
LORA = 512
LT = LORA // P
ROPE = 64
VD = 128
SM_SCALE = (128 + ROPE) ** -0.5
EPS = 1e-6
D_FF = 5632
FT = D_FF // P
PARTS = (32, 12)
UNIT = P
CH = 8 * UNIT
RING = 4
EARLY_RING = 2 * RING
GRID_W = 64

C_DQKV = 0
N_DQKV = 2 * 9
C_HEAD = C_DQKV + N_DQKV
N_HEAD = 2 * HEADS
C_WO = C_HEAD + N_HEAD
C_FFN0 = C_WO + 2 * KT
N_FFN = FT * 4 + FT * KT // 8
C_FNO = C_FFN0 + N_FFN
C_FFN1 = C_FNO + 2 * KT
N_CHUNKS = C_FFN1 + N_FFN

SH1, SC1, G1, SH2, SC2, G2 = range(6)
ADA_BLOCKS = [(G1, 1), (SC2, 1), (SH2, 1), (G2, 2), (6 + SC1, 2), (6 + SH2, 1), (6 + SC2, 1), (6 + G2, 1)]
B_DQKV, B_HEADS, B_WO, B_UP0, B_DOWN0, B_PART0, B_FNO, B_UP1 = range(8)
ADA_AT = [0]
for _first, _n in ADA_BLOCKS:
    ADA_AT.append(ADA_AT[-1] + 32 * _n)
N_ADA = ADA_AT[-1]
MODS_EARLY = 2
HALVES = 4
N_EARLY = HALVES * KT


def backbone(nc, xT, ctxT, cond, ada_early, ada_late, ada_b, gains, lat_gains, weights, conv, consts, rope,
             dft, outT):
    f32, f32r = mybir.dt.float32, mybir.dt.float32r
    ALU, ACT, AX = mybir.AluOpType, mybir.ActivationFunctionType, mybir.AxisListType
    es = ExitStack()
    with es:
        base = -(-nc.sbuf_base // 64) * 64
        room = nc.sbuf_usable_end - base
        es.enter_context(nc.sbuf_tensor("arena", [P, (room - 64) // 4], f32))
        cursor = [0]

        def at(name, shape, dtype, offset):
            return nc.alloc_sbuf_tensor_at(name, shape, dtype, offset=base + offset)

        def place(name, shape, dtype=f32):
            offset = cursor[0]
            cursor[0] += -(-4 * int(np.prod(shape[1:])) // 32) * 32
            assert cursor[0] <= room - 64, (name, cursor[0], room)
            return at(name, shape, dtype, offset)

        x = place("x", [P, KT, SEQ])
        h_hi = place("h_hi", [P, KT, SEQ], f32r)
        h_at = cursor[0]
        h_lo = place("h_lo", [P, KT, SEQ], f32r)
        h_pre = at("h_pre", [P, KT, SEQ], f32, h_at)
        early = at("early", [P, EARLY_RING, CH], f32, cursor[0])
        raw = place("raw", [P, RING, CH])
        ada = place("ada", [P, RING, CH])
        w_hi = place("w_hi", [P, RING, CH], f32r)
        w_lo = place("w_lo", [P, RING, CH], f32r)
        acc0 = place("acc0", [P, D])
        rs_at = cursor[0]
        rstd = place("rstd", [P, NTOK])
        sq = place("sq", [P, NTOK])
        sqt_at = cursor[0]
        sqt = place("sqt", [P, 2, SEQ])
        conv_at = cursor[0]
        conv_s = place("conv_s", [P, 2 * FT, 4])
        const_s = place("const_s", [P, 2, P])
        mod = place("mod", [P, 12, KT])
        mod_c = place("mod_c", [P, 2, KT])
        bias_s = place("bias_s", [P, 12, KT])
        gain_s = place("gain_s", [P, 5, KT])
        lgain_s = place("lgain_s", [P, 2, LT])
        scl = place("scl", [P, 5, KT])
        cond_s = place("cond_s", [P, KT, 2])
        silu_c = place("silu_c", [P, KT, 2])
        silu_s = place("silu_s", [P, KT, 4], f32r)
        mx = place("mx", [P, 2])
        negmax = place("negmax", [P, 2])
        psum_row = place("psum_row", [P, 2])
        rinv = place("rinv", [P, 2])
        warm = place("warm", [P, 1])
        ident, ones = const_s[:, 0, :], const_s[:, 1, :]
        phase_at = cursor[0]

        ckv_hi = place("ckv_hi", [P, LT, NTOK], f32r)
        o = cursor[0]
        ckv_lo = place("ckv_lo", [P, LT, NTOK], f32r)
        ckv = at("ckv", [P, LT, NTOK], f32, o)
        cq_hi = place("cq_hi", [P, LT, SEQ], f32r)
        o = cursor[0]
        cq_lo = place("cq_lo", [P, LT, SEQ], f32r)
        cq = at("cq", [P, LT, SEQ], f32, o)
        kr_hi = place("kr_hi", [P, 2, NTOK], f32r)
        kr_lo = place("kr_lo", [P, 2, NTOK], f32r)
        heads_at = cursor[0]
        qn_hi = place("qn_hi", [P, 2, SEQ], f32r)
        qn_lo = place("qn_lo", [P, 2, SEQ], f32r)
        kn_hi = place("kn_hi", [P, 2, NTOK], f32r)
        kn_lo = place("kn_lo", [P, 2, NTOK], f32r)
        v_hi = place("v_hi", [P, 2, 4, 2 * VD], f32r)
        v_lo = place("v_lo", [P, 2, 4, 2 * VD], f32r)
        qr_hi = place("qr_hi", [P, 2, SEQ], f32r)
        qr_lo = place("qr_lo", [P, 2, SEQ], f32r)
        pt_at = cursor[0]
        pt_hi = place("pt_hi", [P, 4, SEQ], f32r)
        pt_lo = place("pt_lo", [P, 4, SEQ], f32r)
        rope_s = place("rope_s", [P, 2 * SEQ + P + 2])
        cos, sin, rot = rope_s[:, 0:SEQ], rope_s[:, SEQ:2 * SEQ], rope_s[:, 2 * SEQ:2 * SEQ + P]
        pairing = rope_s[0:4, 2 * SEQ + P:]
        early_rows = at("early_rows", [P, HALVES, CH], f32, phase_at)
        hc_hi = at("hc_hi", [P, KT, SEQ], f32r, heads_at)
        ctx_sq = at("ctx_sq", [P, KT, SEQ], f32, heads_at)
        hc_lo = at("hc_lo", [P, KT, SEQ], f32r, heads_at + 4 * KT * SEQ)
        ctx_s = at("ctx_s", [P, KT, SEQ], f32, heads_at + 4 * KT * SEQ)
        kro = at("kro", [P, NTOK], f32, pt_at + 2048)
        krt = at("krt", [P, SEQ], f32, pt_at + 4096)
        assert heads_at + 8 * KT * SEQ <= pt_at + 2048
        prob = at("prob", [P, 2, NTOK], f32, rs_at)
        qraw = at("qraw", [P, SEQ], f32, sqt_at)
        tq = at("tq", [P, SEQ], f32, sqt_at + 4 * SEQ)
        diag = at("diag", [P, 2, P], f32, conv_at)

        cursor[0] = phase_at
        a_hi = place("a_hi", [P, PARTS[0], SEQ], f32r)
        a_lo = place("a_lo", [P, PARTS[0], SEQ], f32r)
        cv = place("cv", [P, 2, 2, SEQ])
        ga = at("ga", [P, SEQ], f32, rs_at + 12 * SEQ)
        acc1 = place("acc1", [P, D])
        cursor[0] = phase_at
        ab_hi = place("ab_hi", [P, 2, 2, 2 * SEQ], f32r)
        cursor[0] = phase_at + 4 * PARTS[1] * SEQ
        dft_hi = place("dft_hi", [P, 2, 3 * SEQ], f32r)
        o = cursor[0]
        dft_lo = place("dft_lo", [P, 2, 3 * SEQ], f32r)
        dft_s = at("dft_s", [P, 2, 3 * SEQ], f32, o)
        assert cursor[0] <= phase_at + 4 * PARTS[0] * SEQ
        ab_lo = place("ab_lo", [P, 2, 2, 2 * SEQ], f32r)
        f_hi = place("f_hi", [P, KT, SEQ], f32r)
        f_lo = place("f_lo", [P, KT, SEQ], f32r)

        bank = [es.enter_context(nc.psum_tensor(f"bank{i}", [P, 512], f32)) for i in range(8)]
        sem = lambda name: es.enter_context(nc.semaphore(name))
        raw_in = [sem(f"raw_in{s}") for s in range(RING)]
        ada_in = [sem(f"ada_in{s}") for s in range(RING)]
        early_in = [sem(f"early_in{s}") for s in range(EARLY_RING)]
        cond_in, x_in, ctx_in, small_in, conv_in, dft_in = (
            sem(n) for n in ("cond_in", "x_in", "ctx_in", "small_in", "conv_in", "dft_in"))
        stored = sem("stored")
        hi_done, lo_done, chunk_used = sem("hi_done"), sem("lo_done"), sem("chunk_used")
        silu_c_done, silu_split, ada_used = sem("silu_c_done"), sem("silu_split"), sem("ada_used")
        early_hi, early_lo, early_used, rows_out, rows_turned = (
            sem(n) for n in ("early_hi", "early_lo", "early_used", "rows_out", "rows_turned"))
        acc_cleared, ada_summed, mod_done, scl_done = (
            sem("acc_cleared"), sem("ada_summed"), sem("mod_done"), sem("scl_done"))
        sq_done, sqt_done, norm_summed, var_done, std_done, rstd_done = (
            sem(n) for n in ("sq_done", "sqt_done", "norm_summed", "var_done", "std_done", "rstd_done"))
        sq0_done, xr_done = sem("sq0_done"), sem("xr_done")
        pre_done, h_hi_done, h_ready = sem("pre_done"), sem("h_hi_done"), sem("h_ready")
        lat_pre, lat_hi, lat_ready = sem("lat_pre"), sem("lat_hi"), sem("lat_ready")
        kr_rot, kr_step, kr_hi_done, kr_ready, kr_zero = (
            sem("kr_rot"), sem("kr_step"), sem("kr_hi_done"), sem("kr_ready"), sem("kr_zero"))
        tile_done, tile_taken, y_done, y_free = sem("tile_done"), sem("tile_taken"), sem("y_done"), sem("y_free")
        proj_done, proj_taken, kq_hi, v_hi_done, rope_step, qr_hi_done, qr_ready = (
            sem(n) for n in ("proj_done", "proj_taken", "kq_hi", "v_hi_done", "rope_step", "qr_hi_done", "qr_ready"))
        s_done, mx_done, negmax_done, exp_done, rinv_done, diag_done = (
            sem(n) for n in ("s_done", "mx_done", "negmax_done", "exp_done", "rinv_done", "diag_done"))
        t_done, pt_hi_done, pt_ready, o_done, o_hi_done, o_taken = (
            sem(n) for n in ("t_done", "pt_hi_done", "pt_ready", "o_done", "o_hi_done", "o_taken"))
        mid_done, left_done, silu_done, gated, a_hi_done, a_ready = (
            sem(n) for n in ("mid_done", "left_done", "silu_done", "gated", "a_hi_done", "a_ready"))
        dft_hi_done, dft_ready, ab_done, ab_hi_done, ab_ready, f_hi_done = (
            sem(n) for n in ("dft_hi_done", "dft_ready", "ab_done", "ab_hi_done", "ab_ready", "f_hi_done"))

        T_UP0, T_DFT = 14, 14 + 2 * FT
        T_UP1 = T_DFT + KT
        Y_WO, Y_FFN0 = 0, KT
        Y_FNO, Y_FFN1 = Y_FFN0 + 2 * KT, Y_FFN0 + 3 * KT
        NRM_KV, NRM_Q, NRM_L0F, NRM_L1, NRM_L1F, NRM_OUT = 2, 3, 4, 5, 6, 7
        H_L0F, H_L1, H_L1F, H_OUT = 32, 48, 64, 80
        SQ_LAT, SQ_ADDS = 12, KT - 1
        FOURIER_AT = (5, 9, 13)
        MOD_G2 = (MODS_EARLY + 4, MODS_EARLY + 8)

        def one(ap):
            return ap.rearrange("p o n -> p (o n)")

        def row(t, i):
            return one(t[:, bass.ds(i, 1), :])

        def proj_index(n):
            return 6 + 4 * n

        def proj_at(n):
            return 3 + 2 * n

        def head_chunk(n):
            return C_HEAD + 3 + 2 * n

        B_K, B_Q, B_V, B_R = 0, 1, (2, 0), 2

        block = es.enter_context(nc.Block())

        @block.sync
        def _(sp):
            def load_chunk(c, slot):
                sp.dma_start(raw[:, slot, :], one(weights[bass.ds(c, 1), :, :].rearrange("o p n -> p o n")))\
                    .then_inc(raw_in[slot], 16)

            def follow_split(c, slot):
                if isinstance(c, int) and c + RING >= N_CHUNKS:
                    return
                sp.wait_ge(lo_done, c + 1)
                load_chunk(c + RING, slot)

            def follow_ada(a, slot):
                if isinstance(a, int) and a + RING >= N_ADA:
                    return
                sp.wait_ge(ada_used, a + 1)
                sp.dma_start(ada[:, slot, :], one(ada_late[bass.ds(a + RING, 1), :, :].rearrange("o p n -> p o n")))\
                    .then_inc(ada_in[slot], 16)

            sp.dma_start(cond_s[:, :, :], cond).then_inc(cond_in, 16)
            sp.dma_start(const_s[:, :, :], consts).then_inc(small_in, 16)
            sp.dma_start(gain_s[:, :, :], gains).then_inc(small_in, 16)
            sp.dma_start(lgain_s[:, :, :], lat_gains).then_inc(small_in, 16)
            sp.dma_start(bias_s[:, :, :], ada_b).then_inc(small_in, 16)
            sp.dma_start(rope_s[:, :], rope).then_inc(small_in, 16)
            sp.dma_start(ctx_s[:, :, :], ctxT).then_inc(ctx_in, 16)
            sp.dma_start(x[:, :, :], xT).then_inc(x_in, 16)
            for e in range(EARLY_RING):
                sp.dma_start(early[:, e, :], ada_early[e, :, :]).then_inc(early_in[e], 16)
            with sp.Fori(1, N_EARLY // EARLY_RING) as i:
                for e in range(EARLY_RING):
                    sp.wait_ge(early_lo, EARLY_RING * (i - 1) + e + 1)
                    sp.dma_start(early[:, e, :], one(ada_early[bass.ds(EARLY_RING * i + e, 1), :, :]
                                                     .rearrange("o p n -> p o n"))).then_inc(early_in[e], 16)
            for c in range(RING):
                sp.wait_ge(early_lo, N_EARLY - EARLY_RING + c + 1)
                load_chunk(c, c)
            for s in range(RING):
                sp.wait_ge(early_lo, N_EARLY - RING + s + 1)
                sp.dma_start(ada[:, s, :], ada_late[s, :, :]).then_inc(ada_in[s], 16)
            for c in range(RING):
                follow_split(c, c % RING)
            a = 0
            for t in range(9):
                for _ in range((5, 4, 2)[(t > 3) + (t > 4)]):
                    follow_ada(a, a % RING)
                    a += 1
                for c in (2 * t + 4, 2 * t + 5):
                    follow_split(c, c % RING)
            for c in (22, 23, 24):
                follow_split(c, c % RING)

            def heads(n0, limit):
                for s in range(4):
                    for e in range(2):
                        follow_ada(ADA_AT[1] + 2 * (n0 + s) + e, (2 * s + e) % RING)
                    for e in range(2):
                        if limit is None or C_HEAD + 7 + 2 * (n0 + s) + e <= limit:
                            follow_split(C_HEAD + 7 + 2 * (n0 + s) + e, (C_HEAD + 7 + 2 * s + e) % RING)

            with sp.Fori(0, 3) as i:
                heads(4 * i, None)
            heads(12, C_WO + 3)
            sp.wait_ge(t_done, 2 * HEADS)
            sp.dma_start(conv_s[:, :, :], conv[0]).then_inc(conv_in, 16)

            def square(c0, b):
                with sp.Fori(0, KT // 2) as i:
                    for t in range(2):
                        for e in range(2):
                            follow_ada(ADA_AT[b] + 4 * i + 2 * t + e, 2 * t + e)
                        for e in range(2):
                            follow_split(c0 + 4 * i + 2 * t + 4 + e, (c0 + 2 * t + e) % RING)

            def ffn(c0, layer):
                def up(c, a):
                    for s in range(2):
                        if a is not None:
                            for e in range(2):
                                follow_ada(a + 2 * s + e, 2 * s + e)
                        for e in range(4):
                            follow_split(c + 4 * s + 4 + e, (c0 + e) % RING)

                if layer == 0:
                    with sp.Fori(0, 16) as i:
                        up(c0 + 8 * i, ADA_AT[B_UP0] + 4 * i)
                else:
                    with sp.Fori(0, 7) as i:
                        up(c0 + 8 * i, ADA_AT[B_UP1] + 4 * i)
                    up(c0 + 56, ADA_AT[B_UP1] + 28)
                    with sp.Fori(8, 16) as i:
                        up(c0 + 8 * i, None)
                c1 = c0 + 4 * PARTS[0]
                with sp.Fori(0, 8) as i:
                    for t in range(2):
                        if layer == 0:
                            for e in range(4):
                                follow_ada(ADA_AT[B_DOWN0] + 8 * i + 4 * t + e, e)
                        for e in range(4):
                            follow_split(c1 + 8 * i + 4 * t + 4 + e, (c1 + e) % RING)
                c2 = c1 + 2 * PARTS[0]
                with sp.Fori(0, PARTS[1] // 2) as i:
                    up(c2 + 8 * i, ADA_AT[B_PART0] + 4 * i if layer == 0 else None)
                c3 = c2 + 4 * PARTS[1]
                if layer == 0:
                    sp.wait_ge(chunk_used, c2)
                    sp.dma_start(dft_s[:, :, :], dft).then_inc(dft_in, 16)
                for t in range(8):
                    if layer == 0:
                        follow_ada(ADA_AT[B_PART0] + 24 + t, t % RING)
                    for c in range(c3 + 3 * t + 4, c3 + 3 * t + 7):
                        follow_split(c, c % RING)

            square(C_WO, B_WO)
            ffn(C_FFN0, 0)
            sp.wait_ge(tile_taken, T_DFT)
            sp.dma_start(conv_s[:, :, :], conv[1]).then_inc(conv_in, 16)
            square(C_FNO, B_FNO)
            ffn(C_FFN1, 1)
            for q in range(4):
                sp.wait_ge(pre_done, H_OUT + 4 * (q + 1))
                sp.dma_start(outT[:, 4 * q:4 * q + 4, :], h_pre[:, 4 * q:4 * q + 4, :]).then_inc(stored, 16)
            sp.wait_ge(stored, 64)

        @block.gpsimd
        def _(pool):
            srcs = [(T, ckv[:, T // 2, (T % 2) * SEQ:(T % 2 + 1) * SEQ], sq[:, (T % 2) * SEQ:(T % 2 + 1) * SEQ])
                    for T in range(8)]
            srcs += [(10 + t, cq[:, t, :], sq[:, 0:SEQ]) for t in range(LT)]
            for n, (T, src, dst) in enumerate(srcs):
                pool.wait_ge(tile_taken, T + 1)
                if T == 10:
                    pool.wait_ge(norm_summed, NRM_KV + 1)
                if n >= 2:
                    pool.wait_ge(sq_done, n - 1)
                pool.tensor_tensor(sqt[:, n % 2, :], src, src, ALU.mult).then_inc(sqt_done, 1)
                pool.wait_ge(sqt_done, n + 1)
                if T in (0, 1, 10):
                    pool.tensor_copy(dst, sqt[:, n % 2, :]).then_inc(sq_done, 1)
                else:
                    pool.wait_ge(sq_done, n)
                    pool.tensor_tensor(dst, dst, sqt[:, n % 2, :], ALU.add).then_inc(sq_done, 1)

            def residual_squares(Y0, round_, after):
                pool.wait_ge(*after)
                t0, a0 = SQ_LAT + KT * round_, SQ_LAT + SQ_ADDS * round_

                def square_of(m, s):
                    pool.wait_ge(y_free, 2 + Y0 + m + 1)
                    xm = row(x, m)
                    pool.tensor_tensor(sqt[:, s, :], xm, xm, ALU.mult).then_inc(sqt_done, 1)

                def add(m, s):
                    pool.wait_ge(sqt_done, t0 + m + 1)
                    pool.wait_ge(sq_done, a0 + m)
                    pool.tensor_tensor(sq[:, 0:SEQ], sq[:, 0:SEQ], sqt[:, s, :], ALU.add).then_inc(sq_done, 1)

                square_of(0, 0)
                pool.wait_ge(sqt_done, t0 + 1)
                pool.tensor_copy(sq[:, 0:SEQ], sqt[:, 0, :]).then_inc(sq_done, 1)
                with pool.Fori(0, KT // 2 - 1) as i:
                    for m, s in ((2 * i + 1, 1), (2 * i + 2, 0)):
                        pool.wait_ge(sq_done, a0 + m - 1)
                        square_of(m, s)
                        add(m, s)
                square_of(KT - 1, 1)

            residual_squares(Y_WO, 0, (o_taken, 1 + HEADS))
            residual_squares(Y_FFN0 + KT, 1, (norm_summed, NRM_L0F + 1))
            residual_squares(Y_FNO, 2, (norm_summed, NRM_L1 + 1))
            residual_squares(Y_FFN1 + KT, 3, (norm_summed, NRM_L1F + 1))

        @block.scalar
        def _(act):
            def split(c, rounds):
                slot = rounds % RING
                act.wait_ge(raw_in[slot], 4 * (c - slot) + 16)
                act.wait_ge(chunk_used, c - RING + 1)
                act.copy(w_hi[:, slot, :], raw[:, slot, :]).then_inc(hi_done, 1)

            act.wait_ge(cond_in, 16)
            act.activation(silu_c[:, :, :], cond_s[:, :, :], ACT.Silu).then_inc(silu_c_done, 1)
            act.wait_ge(silu_c_done, 1)
            act.copy(silu_s[:, :, 0:2], silu_c[:, :, :]).then_inc(silu_split, 1)
            act.wait_ge(ctx_in, 16)
            act.activation(ctx_sq[:, :, :], ctx_s[:, :, :], ACT.Square).then_inc(sq0_done, 1)
            act.wait_ge(x_in, 16)
            act.activation(h_pre[:, :, :], x[:, :, :], ACT.Square).then_inc(sq0_done, 1)

            def std(k, cols):
                act.wait_ge(var_done, k)
                act.activation(rstd[:, 0:cols], rstd[:, 0:cols], ACT.Sqrt).then_inc(std_done, 1)

            def early_bodies(h, work):
                if h == 0:
                    for i in range(2):
                        work(i)
                else:
                    with act.Fori(2 * h, 2 * h + 2) as i:
                        work(i)

            def early_round(i):
                for s in range(EARLY_RING):
                    e = EARLY_RING * i + s
                    act.wait_ge(early_in[s], 16 * (i + 1))
                    if not (isinstance(e, int) and e < RING):
                        act.wait_ge(early_used, e - RING + 1)
                    act.copy(w_hi[:, s % RING, :], early[:, s, :]).then_inc(early_hi, 1)

            for h in range(HALVES):
                early_bodies(h, early_round)
                if h == 1:
                    std(1, NTOK)
                for e in range(2):
                    act.wait_ge(early_used, KT * (h + 1))
                    act.copy(early_rows[0:4, h, e * 512:(e + 1) * 512], bank[2 * (h % 3) + e][0:4, :])\
                        .then_inc(rows_out, 1)
            for c in range(RING):
                act.wait_ge(raw_in[c], 16)
                act.wait_ge(early_used, N_EARLY - RING + c + 1)
                act.copy(w_hi[:, c, :], raw[:, c, :]).then_inc(hi_done, 1)
            for m in range(2 * KT):
                act.wait_ge(pre_done, m + 1)
                dst, src = (hc_hi, ctx_s) if m < KT else (h_hi, h_pre)
                act.copy(dst[:, m % KT, :], src[:, m % KT, :]).then_inc(h_hi_done, 1)
            for t in range(9):
                for c in (2 * t + 4, 2 * t + 5):
                    split(c, c)
                if t == 4:
                    std(2, NTOK)
                if t == 5:
                    for m in range(LT):
                        act.wait_ge(lat_pre, m + 1)
                        act.copy(ckv_hi[:, m, :], ckv[:, m, :]).then_inc(lat_hi, 1)
                if t == 6:
                    act.wait_ge(kr_step, 3)
                    act.copy(kr_hi[0:ROPE, 0, :], kro[0:ROPE, :]).then_inc(kr_hi_done, 1)
                    act.copy(kr_hi[ROPE:P, 1, :], kro[ROPE:P, :]).then_inc(kr_hi_done, 1)
            std(3, SEQ)
            for m in range(LT):
                act.wait_ge(lat_pre, LT + m + 1)
                act.copy(cq_hi[:, m, :], cq[:, m, :]).then_inc(lat_hi, 1)

            def v_evac(buf, n_proj, c):
                for e, after in enumerate(((proj_done, n_proj), (chunk_used, c + 1))):
                    act.wait_ge(*after)
                    act.copy(v_hi[:, buf, 2 * e:2 * e + 2, :], bank[B_V[e]][:, :].rearrange("p (t n) -> p t n", t=2))\
                        .then_inc(v_hi_done, 1)

            def kq_evac(buf, n_proj, c):
                act.wait_ge(proj_done, n_proj)
                act.copy(kn_hi[:, buf, :], bank[B_K][:, :]).then_inc(kq_hi, 1)
                act.wait_ge(chunk_used, c + 1)
                act.copy(qn_hi[:, buf, :], bank[B_Q][:, 0:SEQ]).then_inc(kq_hi, 1)

            def qr_evac(p, buf):
                act.wait_ge(rope_step, 3 * p + 3)
                act.copy(qr_hi[:, buf, :], tq[:, :]).then_inc(qr_hi_done, 1)

            def exps(n):
                for qt in range(2):
                    act.wait_ge(negmax_done, 2 * n + qt + 1)
                    act.activation(prob[:, qt, :], bank[4 + qt][:, :], ACT.Exp, bias=negmax[:, qt:qt + 1],
                                   scale=SM_SCALE, accum_out=psum_row[:, qt:qt + 1]).then_inc(exp_done, 1)

            v_evac(0, 1, C_HEAD)
            split(22, 22)
            split(23, 23)
            kq_evac(0, 2, C_HEAD + 2)
            split(24, 24)
            qr_evac(0, 0)
            exps(0)

            def step(n, s, p, last, top):
                odd, c = s % 2, head_chunk(n)
                if odd or last == 1:
                    if top is None or c + 4 <= top:
                        split(c + 4, C_HEAD + 7 + 2 * s)
                if last < 1:
                    kq_evac((s + 1) % 2, proj_at(n) + 1, c + odd)
                if not odd and (top is None or c + 4 <= top):
                    split(c + 4, C_HEAD + 7 + 2 * s)
                if odd and (top is None or c + 5 <= top):
                    split(c + 5, C_HEAD + 8 + 2 * s)
                if last < 0 and odd:
                    qr_evac(p, (s // 2 + 1) % 2)
                for qt in range(2):
                    act.wait_ge(t_done, 2 * n + qt + 1)
                    act.copy(pt_hi[:, :, qt * P:(qt + 1) * P], bank[6 + qt][:, :].rearrange("p (t n) -> p t n", t=4))\
                        .then_inc(pt_hi_done, 1)
                if last < 0 and not odd:
                    v_evac((s // 2 + 1) % 2, proj_at(n) + 2, c + 1)
                if not odd and (top is None or c + 5 <= top):
                    split(c + 5, C_HEAD + 8 + 2 * s)
                if last < 1:
                    exps(n + 1)
                act.wait_ge(o_done, n + 1)
                act.copy(row(h_hi, n), bank[3][:, 0:SEQ]).then_inc(o_hi_done, 1)

            with act.Fori(0, 3) as i:
                for s in range(4):
                    step(4 * i + s, s, 2 * i + (s + 1) // 2, -1, None)
            for s in range(4):
                step(12 + s, s, 6 + (s + 1) // 2, (s > 1) + (s > 2) - 1, C_WO + 3)

            def load_sqrt():
                act.activation(warm[:, :], ones[:, 0:1], ACT.Sqrt)

            def square(c0):
                load_sqrt()
                with act.Fori(0, KT // 2) as i:
                    for e in range(4):
                        split(c0 + 4 * i + 4 + e, c0 + e)

            def normed(k, h0, shift, between=None):
                std(k, SEQ)
                for m in range(KT):
                    act.wait_ge(pre_done, h0 + m + 1)
                    act.activation(h_hi[:, m, :], h_pre[:, m, :], ACT.Identity, bias=mod[:, shift, m:m + 1])\
                        .then_inc(h_hi_done, 1)
                    if between:
                        between(m)

            def ffn(c0, T0, P0, layer):
                def pair(c, T, Pn, f, j, s):
                    split(c + 4, c0)
                    split(c + 5, c0 + 1)
                    for g in range(2):
                        act.wait_ge(chunk_used, c + 2 * g + 2)
                        taps = conv_s[:, bass.ds(2 * f + g, 1), :]
                        act.activation(cv[:, s, g, :], bank[(T0 + 2 * s + g) % 4][:, 0:SEQ], ACT.Identity,
                                       bias=taps[:, :, 3], scale=taps[:, :, 1]).then_inc(mid_done, 1)
                        split(c + 6 + g, c0 + 2 + g)
                    act.wait_ge(tile_taken, T + 2)
                    act.activation(cv[:, s, 1, :], cv[:, s, 1, :], ACT.Silu).then_inc(silu_done, 1)
                    act.wait_ge(gated, Pn + 1)
                    act.copy(row(a_hi, j), ga[:, :]).then_inc(a_hi_done, 1)

                act.wait_ge(conv_in, 16 * (layer + 1))
                with act.Fori(0, PARTS[0] // 2) as i:
                    for s in range(2):
                        j = 2 * i + s
                        pair(c0 + 8 * i + 4 * s, T0 + 4 * i + 2 * s, P0 + j, j, j, s)
                c1 = c0 + 4 * PARTS[0]
                with act.Fori(0, KT // 2) as i:
                    for e in range(8):
                        split(c1 + 8 * i + 4 + e, c1 + e)
                c2 = c1 + 2 * PARTS[0]
                with act.Fori(0, PARTS[1] // 2) as i:
                    for s in range(2):
                        j = 2 * i + s
                        pair(c2 + 8 * i + 4 * s, T0 + 2 * PARTS[0] + 4 * i + 2 * s, P0 + PARTS[0] + j,
                             PARTS[0] + j, j, s)
                load_sqrt()
                c3 = c2 + 4 * PARTS[1]
                for c in range(c3 + 4, c3 + 28):
                    if c < N_CHUNKS:
                        split(c, c)

            square(C_WO)
            normed(4, H_L0F, SH2)
            ffn(C_FFN0, T_UP0, 0, 0)

            def spectrum(g):
                for t in range(2):
                    act.wait_ge(ab_done, 2 * g + t + 1)
                    act.copy(ab_hi[:, g % 2, t, :], bank[4 + t][:, :]).then_inc(ab_hi_done, 1)

            def back(g):
                for m in (2 * g, 2 * g + 1):
                    act.wait_ge(tile_done, 5 + m + 1)
                    act.copy(f_hi[:, m, :], bank[(T_DFT + m) % 4][:, 0:SEQ]).then_inc(f_hi_done, 1)

            def fourier(g):
                if g < 8:
                    spectrum(g)
                if g:
                    back(g - 1)

            def start_fourier(m):
                if m in FOURIER_AT:
                    fourier(FOURIER_AT.index(m))

            normed(5, H_L1, 6 + SH1, start_fourier)
            for g in range(len(FOURIER_AT), 9):
                fourier(g)
            square(C_FNO)
            normed(6, H_L1F, 6 + SH2)
            ffn(C_FFN1, T_UP1, FT, 1)
            std(7, SEQ)

        @block.vector
        def _(dve):
            def split(c, slot):
                dve.wait_ge(hi_done, c + 1)
                dve.tensor_tensor(w_lo[:, slot, :], raw[:, slot, :], w_hi[:, slot, :].bitcast(f32), ALU.subtract)\
                    .then_inc(lo_done, 1)

            def lo_of(dst, src, hi_part, done):
                dve.tensor_tensor(dst, src, hi_part.bitcast(f32), ALU.subtract).then_inc(done, 1)

            def clear_accs(b):
                if b:
                    dve.wait_ge(ada_summed, b)
                n0 = ADA_AT[b] // 32
                for n, acc in enumerate((acc0, acc1)[:ADA_BLOCKS[b][1]]):
                    dve.memset(acc[:, :], 0.0).then_inc(acc_cleared, 1)
                dve.wait_ge(acc_cleared, n0 + n + 1)

            def ada_step(b, k, e, a):
                both = ADA_BLOCKS[b][1] == 2
                width = 4 if both else 2
                slot = e % RING
                dve.wait_ge(ada_in[slot], 4 * (a - slot) + 16)
                if not (isinstance(a, int) and a < width):
                    dve.wait_ge(ada_used, a - width + 1)
                acc = (acc0, acc1)[(e % width) // 2]
                part = acc[:, (e % 2) * CH:(e % 2 + 1) * CH]
                dve.scalar_tensor_tensor(part, ada[:, slot, :], one(silu_c[:, bass.ds(k, 1), 0:1]), part,
                                         ALU.mult, ALU.add).then_inc(ada_used, 1)

            def mods(b):
                first, n = ADA_BLOCKS[b]
                dve.wait_ge(ada_summed, b + 1)
                dve.tensor_tensor(mod[:, first:first + n, :], bank[7][:, 0:n * KT].rearrange("p (n k) -> p n k", n=n),
                                  bias_s[:, first:first + n, :], ALU.add).then_inc(mod_done, 1)

            def scales(i, scale, gain, need):
                dve.wait_ge(mod_done, need)
                dve.scalar_tensor_tensor(scl[:, i, :], scale, 1.0, gain_s[:, gain, :], ALU.add, ALU.mult)\
                    .then_inc(scl_done, 1)

            def invert(k, cols):
                dve.wait_ge(std_done, k)
                dve.reciprocal(rstd[:, 0:cols], rstd[:, 0:cols]).then_inc(rstd_done, 1)
                dve.wait_ge(rstd_done, k)

            dve.memset(mx[:, :], 0.0).then_inc(y_free, 2)
            dve.memset(negmax[:, :], 0.0).then_inc(o_taken, 1)
            dve.wait_ge(small_in, 16 * 5)
            dve.wait_ge(silu_split, 1)
            dve.tensor_tensor(silu_s[:, :, 2:4], silu_c[:, :, :], silu_s[:, :, 0:2].bitcast(f32), ALU.subtract)\
                .then_inc(silu_split, 1)

            def early_split(e, slot):
                dve.wait_ge(early_hi, e + 1)
                dve.tensor_tensor(w_lo[:, slot % RING, :], early[:, slot, :], w_hi[:, slot % RING, :].bitcast(f32),
                                  ALU.subtract).then_inc(early_lo, 1)

            with dve.Fori(0, 3) as i:
                for e in range(EARLY_RING):
                    early_split(EARLY_RING * i + e, e)
            dve.wait_ge(norm_summed, 2)
            dve.tensor_scalar(rstd[:, :], bank[6][:, :], 1.0 / D, EPS, ALU.mult, ALU.add).then_inc(var_done, 1)
            for e in range(EARLY_RING):
                early_split(3 * EARLY_RING + e, e)
            invert(1, NTOK)
            with dve.Fori(4, 8) as i:
                for e in range(EARLY_RING):
                    early_split(EARLY_RING * i + e, e)
                    if e % 2 == 0:
                        m = 4 * (i - 4) + e // 2
                        for t, cols in ((ctx_s, slice(0, SEQ)), (x, slice(SEQ, NTOK))):
                            dst = ctx_s if t is ctx_s else h_pre
                            dve.tensor_tensor(row(dst, m), row(t, m), rstd[:, cols], ALU.mult).then_inc(xr_done, 1)
            dve.wait_ge(rows_turned, HALVES)
            first = bank[7][:, 0:2 * 2 * KT].rearrange("p (m k s) -> p m k s", m=2, s=2)
            dve.tensor_tensor(mod_c[:, :, :], first[:, :, :, 1], bias_s[:, 0:2, :], ALU.add).then_inc(mod_done, 1)
            dve.tensor_tensor(mod[:, 0:2, :], first[:, :, :, 0], bias_s[:, 0:2, :], ALU.add).then_inc(mod_done, 1)
            scales(1, mod_c[:, SC1, :], 0, MODS_EARLY)
            scales(0, mod[:, SC1, :], 0, MODS_EARLY)
            for c in range(RING):
                split(c, c)
            dve.wait_ge(scl_done, 2)
            dve.wait_ge(xr_done, 2 * KT)

            def first_pre(m):
                src, s, md = (ctx_s, 1, mod_c) if m < KT else (h_pre, 0, mod)
                k = m % KT
                dve.tensor_scalar(src[:, k, :], src[:, k, :], scl[:, s, k:k + 1], md[:, SH1, k:k + 1],
                                  ALU.mult, ALU.add).then_inc(pre_done, 1)

            def first_lo(m):
                dst, src, hi_part = (hc_lo, ctx_s, hc_hi) if m < KT else (h_lo, h_pre, h_hi)
                dve.wait_ge(h_hi_done, m + 1)
                lo_of(dst[:, m % KT, :], src[:, m % KT, :], hi_part[:, m % KT, :], h_ready)

            for m in range(2 * KT + 2):
                if m < 2 * KT:
                    first_pre(m)
                if m >= 2:
                    first_lo(m - 2)

            clear_accs(0)
            a = 0
            for t in range(9):
                if t < 5:
                    for e in range(2):
                        T = 2 * t + e
                        dve.wait_ge(*((chunk_used, 2 * t + 2) if e else (tile_done, t + 1)))
                        dst = ckv[:, t, e * SEQ:(e + 1) * SEQ] if t < 4 else kro[:, e * SEQ:(e + 1) * SEQ]
                        dve.tensor_copy(dst, bank[T % 4][:, 0:SEQ]).then_inc(tile_taken, 1)
                else:
                    T = 10 + t - 5
                    dve.wait_ge(chunk_used, 2 * t + 2)
                    dve.tensor_copy(cq[:, t - 5, :], bank[T % 4][:, 0:SEQ]).then_inc(tile_taken, 1)
                for _ in range((5, 4, 2)[(t > 3) + (t > 4)]):
                    ada_step(0, a // 2, a % 4, a)
                    a += 1
                for c in (2 * t + 4, 2 * t + 5):
                    split(c, c % RING)
                if t == 4:
                    dve.wait_ge(norm_summed, NRM_KV + 1)
                    dve.tensor_scalar(rstd[:, :], bank[6][:, :], 1.0 / LORA, EPS, ALU.mult, ALU.add)\
                        .then_inc(var_done, 1)
                    invert(2, NTOK)
                    for m in range(LT):
                        dve.scalar_tensor_tensor(ckv[:, m, :], ckv[:, m, :], lgain_s[:, 1, m:m + 1], rstd[:, :],
                                                 ALU.mult, ALU.mult).then_inc(lat_pre, 1)
                if t == 5:
                    for m in range(LT):
                        dve.wait_ge(lat_hi, m + 1)
                        lo_of(ckv_lo[:, m, :], ckv[:, m, :], ckv_hi[:, m, :], lat_ready)
                    dve.wait_ge(kr_rot, 1)
                    dve.tensor_tensor(krt[:, :], bank[7][:, 0:SEQ], sin, ALU.mult).then_inc(kr_step, 1)
                    dve.tensor_tensor(kro[:, SEQ:NTOK], kro[:, SEQ:NTOK], cos, ALU.mult).then_inc(kr_step, 1)
                    dve.wait_ge(kr_step, 2)
                    dve.tensor_tensor(kro[:, SEQ:NTOK], kro[:, SEQ:NTOK], krt[:, :], ALU.add).then_inc(kr_step, 1)
                    dve.memset(kr_hi[ROPE:P, 0, :].bitcast(f32), 0.0).then_inc(kr_zero, 1)
                    dve.memset(kr_lo[ROPE:P, 0, :].bitcast(f32), 0.0).then_inc(kr_zero, 1)
                    dve.memset(kr_hi[0:ROPE, 1, :].bitcast(f32), 0.0).then_inc(kr_zero, 1)
                    dve.memset(kr_lo[0:ROPE, 1, :].bitcast(f32), 0.0).then_inc(kr_zero, 1)
                if t == 6:
                    dve.wait_ge(kr_hi_done, 1)
                    lo_of(kr_lo[0:ROPE, 0, :], kro[0:ROPE, :], kr_hi[0:ROPE, 0, :], kr_ready)
                    dve.wait_ge(kr_hi_done, 2)
                    lo_of(kr_lo[ROPE:P, 1, :], kro[ROPE:P, :], kr_hi[ROPE:P, 1, :], kr_ready)
            dve.wait_ge(norm_summed, NRM_Q + 1)
            dve.tensor_scalar(rstd[:, 0:SEQ], bank[6][:, 0:SEQ], 1.0 / LORA, EPS, ALU.mult, ALU.add)\
                .then_inc(var_done, 1)
            invert(3, SEQ)
            for m in range(LT):
                dve.scalar_tensor_tensor(cq[:, m, :], cq[:, m, :], lgain_s[:, 0, m:m + 1], rstd[:, 0:SEQ],
                                         ALU.mult, ALU.mult).then_inc(lat_pre, 1)
            for m in range(LT):
                dve.wait_ge(lat_hi, LT + m + 1)
                lo_of(cq_lo[:, m, :], cq[:, m, :], cq_hi[:, m, :], lat_ready)
            mods(0)

            def v_lo_parts(v_count, buf):
                for e in range(2):
                    dve.wait_ge(v_hi_done, v_count + e + 1)
                    lo_of(v_lo[:, buf, 2 * e:2 * e + 2, :], bank[B_V[e]][:, :].rearrange("p (t n) -> p t n", t=2),
                          v_hi[:, buf, 2 * e:2 * e + 2, :], proj_taken)

            def kq_lo_parts(n, buf):
                dve.wait_ge(kq_hi, 2 * n + 1)
                lo_of(kn_lo[:, buf, :], bank[B_K][:, :], kn_hi[:, buf, :], proj_taken)
                dve.wait_ge(kq_hi, 2 * n + 2)
                lo_of(qn_lo[:, buf, :], bank[B_Q][:, 0:SEQ], qn_hi[:, buf, :], proj_taken)

            def rope_take(c):
                dve.wait_ge(chunk_used, c + 1)
                dve.tensor_copy(qraw[:, :], bank[B_R][:, 0:SEQ]).then_inc(proj_taken, 1)

            def rope_turn(p, q, n_proj):
                dve.wait_ge(proj_taken, q + 1)
                dve.tensor_tensor(tq[:, :], qraw[:, :], cos, ALU.mult).then_inc(rope_step, 1)
                dve.wait_ge(proj_done, n_proj)
                dve.wait_ge(rope_step, 3 * p + 1)
                dve.tensor_tensor(qraw[:, :], bank[B_R][:, 0:SEQ], sin, ALU.mult).then_inc(proj_taken, 1)
                dve.wait_ge(proj_taken, q + 4)
                dve.tensor_tensor(tq[:, :], tq[:, :], qraw[:, :], ALU.add).then_inc(rope_step, 2)

            def rope_lo(p, buf):
                dve.wait_ge(qr_hi_done, p + 1)
                lo_of(qr_lo[:, buf, :], tq[:, :], qr_hi[:, buf, :], qr_ready)

            def maxima(n):
                for qt in range(2):
                    dve.wait_ge(s_done, 2 * n + qt + 1)
                    dve.reduce_max(mx[:, qt:qt + 1], bank[4 + qt][:, :], axis=AX.X).then_inc(mx_done, 1)
                    dve.wait_ge(mx_done, 2 * n + qt + 1)
                    dve.tensor_scalar(negmax[:, qt:qt + 1], mx[:, qt:qt + 1], -SM_SCALE, None, ALU.mult)\
                        .then_inc(negmax_done, 1)

            v_lo_parts(0, 0)
            split(22, 22 % RING)
            rope_take(C_HEAD + 1)
            split(23, 23 % RING)
            kq_lo_parts(0, 0)
            rope_turn(0, 2, 3)
            rope_lo(0, 0)
            split(24, 24 % RING)
            clear_accs(1)
            maxima(0)

            def step(n, s, p, last, top):
                q, c, odd = proj_index(n), head_chunk(n), s % 2
                first, second = [(C_HEAD + 7 + 2 * s + e) % RING for e in range(2)]
                for e in range(2):
                    ada_step(1, n, 2 * s + e, ADA_AT[1] + 2 * n + e)
                if odd and last < 0:
                    rope_take(c)
                if odd and (top is None or c + 4 <= top):
                    split(c + 4, first)
                if last < 1:
                    kq_lo_parts(n + 1, (s + 1) % 2)
                dve.wait_ge(exp_done, 2 * n + 2)
                dve.reciprocal(rinv[:, :], psum_row[:, :]).then_inc(rinv_done, 1)
                dve.wait_ge(rinv_done, n + 1)
                for qt in range(2):
                    dve.tensor_scalar(diag[:, qt, :], ident, rinv[:, qt:qt + 1], None, ALU.mult).then_inc(diag_done, 1)
                if odd and last < 0:
                    rope_turn(p, q, proj_at(n) + 2)
                if top is None or c + 4 + odd <= top:
                    split(c + 4 + odd, second if odd else first)
                if odd and last < 0:
                    rope_lo(p, (s // 2 + 1) % 2)
                for qt in range(2):
                    dve.wait_ge(pt_hi_done, 2 * n + qt + 1)
                    lo_of(pt_lo[:, :, qt * P:(qt + 1) * P], bank[6 + qt][:, :].rearrange("p (t n) -> p t n", t=4),
                          pt_hi[:, :, qt * P:(qt + 1) * P], pt_ready)
                if not odd:
                    if last < 0:
                        v_lo_parts(n + 2, (s // 2 + 1) % 2)
                    if top is None or c + 5 <= top:
                        split(c + 5, second)
                if last < 1:
                    maxima(n + 1)
                dve.wait_ge(o_hi_done, n + 1)
                lo_of(row(h_lo, n), bank[3][:, 0:SEQ], row(h_hi, n), o_taken)

            with dve.Fori(0, 3) as i:
                for s in range(4):
                    step(4 * i + s, s, 2 * i + (s + 1) // 2, -1, None)
            for s in range(4):
                step(12 + s, s, 6 + (s + 1) // 2, (s > 1) + (s > 2) - 1, C_WO + 3)
            mods(1)
            scales(2, mod[:, SC2, :], 2, MODS_EARLY + 2)
            clear_accs(B_WO)

            def residual(m, e, gate, *after):
                dve.wait_ge(*after)
                xm = row(x, m)
                g = one(mod[:, gate:gate + 1, bass.ds(m, 1)])
                dve.scalar_tensor_tensor(xm, bank[4 + e][:, 0:SEQ], g, xm, ALU.mult, ALU.add).then_inc(y_free, 1)

            def square(c0, b, gate):
                with dve.Fori(0, KT // 2) as i:
                    for t in range(2):
                        m, c = 2 * i + t, c0 + 4 * i + 2 * t
                        for e in range(2):
                            ada_step(b, m, 2 * t + e, ADA_AT[b] + 4 * i + 2 * t + e)
                        split(c + 4, (c0 + 2 * t) % RING)
                        residual(m, t, gate, chunk_used, c + 2)
                        split(c + 5, (c0 + 2 * t + 1) % RING)

            def norm(k, n_sum):
                dve.wait_ge(norm_summed, n_sum + 1)
                dve.tensor_scalar(rstd[:, 0:SEQ], bank[6][:, 0:SEQ], 1.0 / D, EPS, ALU.mult, ALU.add)\
                    .then_inc(var_done, 1)
                invert(k, SEQ)

            def normed(k, n_sum, h0, i, shift, results=None, between=None):
                norm(k, n_sum)
                if results:
                    results()
                for m in range(KT + 2):
                    if m < KT:
                        dve.scalar_tensor_tensor(h_pre[:, m, :], x[:, m, :], scl[:, i, m:m + 1], rstd[:, 0:SEQ],
                                                 ALU.mult, ALU.mult).then_inc(pre_done, 1)
                    if m >= 2:
                        j = m - 2
                        dve.wait_ge(h_hi_done, h0 + j + 1)
                        dve.scalar_tensor_tensor(h_lo[:, j, :], h_pre[:, j, :], mod[:, shift, j:j + 1],
                                                 h_hi[:, j, :].bitcast(f32), ALU.add, ALU.subtract).then_inc(h_ready, 1)
                    if between:
                        between(m)

            def ffn(c0, T0, P0, layer):
                dve.wait_ge(conv_in, 16 * (layer + 1))

                def pair(c, Pn, f, j, s):
                    split(c + 4, c0 % RING)
                    split(c + 5, (c0 + 1) % RING)
                    for g in range(2):
                        t, b = conv_s[:, bass.ds(2 * f + g, 1), :], bank[(T0 + 2 * s + g) % 4]
                        v = cv[:, s, g, :]
                        dve.wait_ge(mid_done, 2 * Pn + g + 1)
                        dve.scalar_tensor_tensor(v[:, 1:SEQ], b[:, 0:SEQ - 1], t[:, :, 0], v[:, 1:SEQ],
                                                 ALU.mult, ALU.add).then_inc(left_done, 1)
                        dve.wait_ge(left_done, 2 * Pn + g + 1)
                        dve.scalar_tensor_tensor(v[:, 0:SEQ - 1], b[:, 1:SEQ], t[:, :, 2], v[:, 0:SEQ - 1],
                                                 ALU.mult, ALU.add).then_inc(tile_taken, 1)
                        split(c + 6 + g, (c0 + 2 + g) % RING)
                    dve.wait_ge(silu_done, Pn + 1)
                    dve.tensor_tensor(ga[:, :], cv[:, s, 0, :], cv[:, s, 1, :], ALU.mult).then_inc(gated, 1)
                    dve.wait_ge(a_hi_done, Pn + 1)
                    lo_of(row(a_lo, j), ga[:, :], row(a_hi, j), a_ready)

                def up(i, c, Pn, f, ada_ops):
                    for s in range(2):
                        ada_ops(i, s)
                        pair(c + 8 * i + 4 * s, Pn + 2 * i + s, f + 2 * i + s, 2 * i + s, s)

                def both(i, s):
                    for e in range(2):
                        ada_step(B_UP0, i, 2 * s + e, ADA_AT[B_UP0] + 4 * i + 2 * s + e)

                def single(b):
                    def ops(i, s):
                        for e in range(2):
                            ada_step(b, 2 * i + s, 2 * s + e, ADA_AT[b] + 4 * i + 2 * s + e)
                    return ops

                def none(i, s):
                    pass

                if layer == 0:
                    with dve.Fori(0, 16) as i:
                        up(i, c0, P0, 0, both)
                    mods(B_UP0)
                    clear_accs(B_DOWN0)
                else:
                    with dve.Fori(0, 8) as i:
                        up(i, c0, P0, 0, single(B_UP1))
                    with dve.Fori(8, 16) as i:
                        up(i, c0, P0, 0, none)
                    mods(B_UP1)
                gate = 6 * layer + G2
                dve.wait_ge(mod_done, MOD_G2[layer])
                c1 = c0 + 4 * PARTS[0]
                with dve.Fori(0, KT // 2) as i:
                    for t in range(2):
                        m = 2 * i + t
                        if layer == 0:
                            for e in range(4):
                                ada_step(B_DOWN0, m, e, ADA_AT[B_DOWN0] + 4 * m + e)
                        for e in range(3):
                            split(c1 + 4 * m + 4 + e, (c1 + e) % RING)
                        residual(m, t, gate, chunk_used, c1 + 4 * m + 4)
                        split(c1 + 4 * m + 7, (c1 + 3) % RING)
                if layer == 0:
                    mods(B_DOWN0)
                    scales(3, mod[:, 6 + SC1, :], 1, MODS_EARLY + B_DOWN0 + 1)
                    clear_accs(B_PART0)
                c2 = c1 + 2 * PARTS[0]
                with dve.Fori(0, PARTS[1] // 2) as i:
                    up(i, c2, P0 + PARTS[0], PARTS[0], single(B_PART0) if layer == 0 else none)
                c3 = c2 + 4 * PARTS[1]
                for t in range(8):
                    if layer == 0:
                        ada_step(B_PART0, 12 + t // 2, t % 4, ADA_AT[B_PART0] + 24 + t)
                        if t == 2:
                            dve.wait_ge(dft_in, 16)
                            dve.tensor_copy(dft_hi[:, :, :], dft_s[:, :, :]).then_inc(dft_hi_done, 1)
                        if t == 3:
                            dve.wait_ge(dft_hi_done, 1)
                            lo_of(dft_lo[:, :, :], dft_s[:, :, :], dft_hi[:, :, :], dft_ready)
                    for e in range(3):
                        if e:
                            residual(2 * t + e - 1, e - 1, gate,
                                     *((chunk_used, c3 + 3 * t + 3) if e == 2 else (y_done, 8 * layer + t + 1)))
                        c = c3 + 3 * t + 4 + e
                        if c < N_CHUNKS:
                            split(c, c % RING)

            dve.wait_ge(mod_done, MODS_EARLY + 1)
            square(C_WO, B_WO, G1)
            dve.wait_ge(scl_done, 3)
            normed(4, NRM_L0F, H_L0F, 2, SH2, lambda: mods(B_WO))
            clear_accs(B_UP0)
            ffn(C_FFN0, T_UP0, 0, 0)
            dve.wait_ge(scl_done, 4)

            def spectrum(g):
                for t in range(2):
                    dve.wait_ge(ab_hi_done, 2 * g + t + 1)
                    lo_of(ab_lo[:, g % 2, t, :], bank[4 + t][:, :], ab_hi[:, g % 2, t, :], ab_ready)

            def back(g):
                for m in (2 * g, 2 * g + 1):
                    dve.wait_ge(f_hi_done, m + 1)
                    lo_of(f_lo[:, m, :], bank[(T_DFT + m) % 4][:, 0:SEQ], f_hi[:, m, :], tile_taken)

            def fourier(g):
                if g < 8:
                    spectrum(g)
                if g:
                    back(g - 1)

            def start_fourier(m):
                if m in FOURIER_AT:
                    fourier(FOURIER_AT.index(m))

            normed(5, NRM_L1, H_L1, 3, 6 + SH1, between=start_fourier)
            for g in range(len(FOURIER_AT), 9):
                fourier(g)
                if g == 5:
                    mods(B_PART0)
                    clear_accs(B_FNO)
            square(C_FNO, B_FNO, 6 + G1)

            def scale_l1f():
                mods(B_FNO)
                scales(4, mod[:, 6 + SC2, :], 3, MODS_EARLY + 7)
                dve.wait_ge(scl_done, 5)

            normed(6, NRM_L1F, H_L1F, 4, 6 + SH2, scale_l1f)
            clear_accs(B_UP1)
            ffn(C_FFN1, T_UP1, FT, 1)
            norm(7, NRM_OUT)
            for m in range(KT):
                dve.scalar_tensor_tensor(h_pre[:, m, :], x[:, m, :], gain_s[:, 4, m:m + 1], rstd[:, 0:SEQ],
                                         ALU.mult, ALU.mult).then_inc(pre_done, 1)

        @block.tensor
        def _(pe):
            def product(out, slot, u, hi_part, lo_part, first, last):
                wh = w_hi[:, slot, u * UNIT:(u + 1) * UNIT]
                wl = w_lo[:, slot, u * UNIT:(u + 1) * UNIT]
                pe.matmul(out, wh, hi_part, start=first, stop=False)
                pe.matmul(out, wh, lo_part, start=False, stop=False)
                return pe.matmul(out, wl, hi_part, start=False, stop=last)

            def moving(out, a_h, a_l, b_h, b_l, first, last):
                pe.matmul(out, a_h, b_h, start=first, stop=False)
                pe.matmul(out, a_h, b_l, start=False, stop=False)
                return pe.matmul(out, a_l, b_h, start=False, stop=last)

            def residual_sum(round_):
                pe.wait_ge(sq_done, SQ_LAT + SQ_ADDS * (round_ + 1))
                pe.matmul(bank[6][:, 0:SEQ], ones, sq[:, 0:SEQ], start=True, stop=False)
                pe.wait_ge(sqt_done, SQ_LAT + KT * (round_ + 1))
                pe.matmul(bank[6][:, 0:SEQ], ones, sqt[:, 1, :], start=False, stop=True)\
                    .then_inc(norm_summed, 1)

            def norm_sum(cols, need):
                pe.wait_ge(sq_done, need)
                pe.matmul(bank[6][:, 0:cols], ones, sq[:, 0:cols], start=True, stop=True)\
                    .then_inc(norm_summed, 1)

            def ada_sum(b):
                pe.wait_ge(ada_used, ADA_AT[b + 1])
                for n in range(ADA_BLOCKS[b][1]):
                    acc = (acc0, acc1)[n]
                    for j in range(KT):
                        mm = pe.matmul(bank[7][:, n * KT + j:n * KT + j + 1], acc[:, j * P:(j + 1) * P],
                                       ones[:, 0:1], start=True, stop=True)
                mm.then_inc(ada_summed, 1)

            pe.wait_ge(small_in, 16 * 5)

            def turn(h):
                pe.wait_ge(rows_out, 2 * h + 2)
                for j in range(8):
                    at_col = 2 * (8 * h + j)
                    mm = pe.matmul(bank[7][:, at_col:at_col + 2], early_rows[0:4, h, j * P:(j + 1) * P], pairing,
                                   start=True, stop=True)
                mm.then_inc(rows_turned, 1)

            pe.wait_ge(silu_split, 2)
            for h in range(HALVES):
                for k in range(KT):
                    e = KT * h + k
                    pe.wait_ge(early_lo, e + 1)
                    for w in (w_hi, w_lo):
                        for b in range(2):
                            mm = pe.matmul(bank[2 * (h % 3) + b][0:4, :], silu_s[:, k, :],
                                           w[:, e % RING, b * 512:(b + 1) * 512],
                                           start=(k == 0 and w is w_hi), stop=(k == KT - 1 and w is w_lo))
                    mm.then_inc(early_used, 1)
                    if h == 0:
                        n, src = (0, ctx_sq) if k < 8 else (1, h_pre)
                        if k % 8 == 0:
                            pe.wait_ge(sq0_done, n + 1)
                        for r in (2 * (k % 8), 2 * (k % 8) + 1):
                            mm = pe.matmul(bank[6][:, n * SEQ:(n + 1) * SEQ], ones, src[:, r, :],
                                           start=(r == 0), stop=(r == KT - 1))
                        if k % 8 == 7:
                            mm.then_inc(norm_summed, 1)
                    if h and k == 3:
                        turn(h - 1)
            turn(HALVES - 1)

            for t in range(9):
                for e in range(2 if t < 5 else 1):
                    T = 2 * t + e if t < 5 else 10 + t - 5
                    context = t < 5 and e == 0
                    hh, hl, h0 = (hc_hi, hc_lo, 0) if context else (h_hi, h_lo, KT)
                    if T >= 4:
                        pe.wait_ge(tile_taken, T - 3)
                    elif T == 0:
                        pe.wait_ge(mod_done, MODS_EARLY)
                    for k in range(KT):
                        c = 2 * t + k // 8
                        if k % 8 == 0:
                            pe.wait_ge(lo_done, c + 1)
                        if t == 0:
                            pe.wait_ge(h_ready, h0 + k + 1)
                        mm = product(bank[T % 4][:, 0:SEQ], c % RING, k % 8, hh[:, k, :], hl[:, k, :],
                                     k == 0, k == KT - 1)
                        if not context and k % 8 == 7:
                            mm.then_inc(chunk_used, 1)
                    if context:
                        mm.then_inc(tile_done, 1)
                if t == 5:
                    norm_sum(NTOK, 8)
                if t == 6:
                    pe.wait_ge(tile_taken, 10)
                    pe.matmul(bank[7][:, 0:SEQ], rot, kro[:, SEQ:NTOK], start=True, stop=True).then_inc(kr_rot, 1)

            def values(buf, slot, c, q):
                pe.wait_ge(lo_done, c + 1)
                for e in range(2):
                    if not (isinstance(q, int) and q == 0):
                        pe.wait_ge(proj_taken, q - 2 + e)
                    for t in range(2):
                        tok = slice((2 * e + t) * P, (2 * e + t + 1) * P)
                        for k in range(LT):
                            w = slice(2 * k * UNIT, 2 * (k + 1) * UNIT)
                            mm = moving(bank[B_V[e]][:, t * 2 * VD:(t + 1) * 2 * VD], ckv_hi[:, k, tok],
                                        ckv_lo[:, k, tok], w_hi[:, slot, w], w_lo[:, slot, w], k == 0, k == LT - 1)
                    mm.then_inc(chunk_used if e else proj_done, 1)

            def keys_queries(slot, c, k_free, q_free):
                pe.wait_ge(lo_done, c + 1)
                pe.wait_ge(proj_taken, k_free)
                for k in range(LT):
                    mm = product(bank[B_K][:, :], slot, k, ckv_hi[:, k, :], ckv_lo[:, k, :], k == 0, k == LT - 1)
                mm.then_inc(proj_done, 1)
                pe.wait_ge(proj_taken, q_free)
                for k in range(LT):
                    mm = product(bank[B_Q][:, 0:SEQ], slot, 4 + k, cq_hi[:, k, :], cq_lo[:, k, :], k == 0, k == LT - 1)
                mm.then_inc(chunk_used, 1)

            def rope_queries(slot, c, q):
                pe.wait_ge(lo_done, c + 1)
                pe.wait_ge(proj_taken, q - 1)
                for k in range(LT):
                    mm = product(bank[B_R][:, 0:SEQ], slot, k, cq_hi[:, k, :], cq_lo[:, k, :], k == 0, k == LT - 1)
                mm.then_inc(chunk_used, 1)

            def rotate(q):
                pe.wait_ge(proj_taken, q + 1)
                pe.matmul(bank[B_R][:, 0:SEQ], rot, qraw[:, :], start=True, stop=True).then_inc(proj_done, 1)

            def scores(n, s):
                buf, pair = s % 2, (s // 2) % 2
                pe.wait_ge(proj_taken, 4 * n + 5 - s % 2)
                for qt in range(2):
                    rows = slice(qt * P, (qt + 1) * P)
                    out = bank[4 + qt][:, :]
                    q_hi, q_lo = qn_hi[:, buf, rows], qn_lo[:, buf, rows]
                    r_hi, r_lo = qr_hi[:, pair, rows], qr_lo[:, pair, rows]
                    pe.matmul(out, q_lo, kn_hi[:, buf, :], start=True, stop=False)
                    pe.matmul(out, q_hi, kn_lo[:, buf, :], start=False, stop=False)
                    pe.matmul(out, r_lo, kr_hi[:, buf, :], start=False, stop=False)
                    pe.matmul(out, r_hi, kr_lo[:, buf, :], start=False, stop=False)
                    pe.matmul(out, r_hi, kr_hi[:, buf, :], start=False, stop=False)
                    pe.matmul(out, q_hi, kn_hi[:, buf, :], start=False, stop=True).then_inc(s_done, 1)

            pe.wait_ge(tile_taken, 14)
            norm_sum(SEQ, SQ_LAT)
            pe.wait_ge(lat_ready, LT)
            values(0, C_HEAD % RING, C_HEAD, 0)
            ada_sum(0)
            pe.wait_ge(lat_ready, 2 * LT)
            rope_queries((C_HEAD + 1) % RING, C_HEAD + 1, 2)
            keys_queries((C_HEAD + 2) % RING, C_HEAD + 2, 2, 0)
            rotate(2)
            pe.wait_ge(kr_ready, 2)
            pe.wait_ge(kr_zero, 4)
            pe.wait_ge(qr_ready, 1)
            scores(0, 0)

            def step(n, s, p, last):
                buf, pair, odd = s % 2, (s // 2) % 2, s % 2
                q, c = proj_index(n), head_chunk(n)
                slots = [(C_HEAD + 3 + 2 * s + e) % RING for e in range(2)]
                if odd and last < 0:
                    rope_queries(slots[0], c, q)
                if last < 1:
                    keys_queries(slots[odd], c + odd, q if odd else q - 2, q - 2 if odd else q - 1)
                if odd and last < 0:
                    rotate(q)
                for qt in range(2):
                    pe.wait_ge(diag_done, 2 * n + qt + 1)
                    for t in range(4):
                        mm = pe.matmul(bank[6 + qt][:, t * P:(t + 1) * P], prob[:, qt, t * P:(t + 1) * P],
                                       diag[:, qt, :], start=True, stop=True)
                    mm.then_inc(t_done, 1)
                if not odd and last < 0:
                    values((s // 2 + 1) % 2, slots[1], c + 1, q + 2)
                if last < 1:
                    if odd:
                        pe.wait_ge(qr_ready, p + 1)
                    scores(n + 1, (s + 1) % 4)
                pe.wait_ge(pt_ready, 2 * n + 2)
                pe.wait_ge(o_taken, n + 1)
                v = slice(buf * VD, (buf + 1) * VD)
                for t in range(4):
                    mm = moving(bank[3][:, 0:SEQ], v_hi[:, pair, t, v], v_lo[:, pair, t, v], pt_hi[:, t, :],
                                pt_lo[:, t, :], t == 0, t == 3)
                mm.then_inc(o_done, 1)

            with pe.Fori(0, 3) as i:
                for s in range(4):
                    step(4 * i + s, s, 2 * i + (s + 1) // 2, -1)
            for s in range(4):
                step(12 + s, s, 6 + (s + 1) // 2, (s > 1) + (s > 2) - 1)
            ada_sum(1)

            def square(c0, Y0, hh, hl):
                with pe.Fori(0, KT // 2) as i:
                    for t in range(2):
                        pe.wait_ge(y_free, Y0 + 2 * i + t + 1)
                        for k in range(KT):
                            e = 2 * t + k // 8
                            if k % 8 == 0:
                                pe.wait_ge(lo_done, c0 + 4 * i + e + 1)
                            mm = product(bank[4 + t][:, 0:SEQ], (c0 + e) % RING, k % 8, hh[:, k, :], hl[:, k, :],
                                         k == 0, k == KT - 1)
                            if k % 8 == 7:
                                mm.then_inc(chunk_used, 1)

            def up(c0, T0, i, h0=None):
                if h0 is not None:
                    pe.wait_ge(lo_done, c0 + 4)
                    for k in range(KT):
                        pe.wait_ge(h_ready, h0 + k + 1)
                        for g in range(2):
                            mm = product(bank[(T0 + g) % 4][:, 0:SEQ], (c0 + 2 * g + k // 8) % RING, k % 8,
                                         h_hi[:, k, :], h_lo[:, k, :], k == 0, k == KT - 1)
                            if k % 8 == 7 and g == 0:
                                mm.then_inc(chunk_used, 1)
                    mm.then_inc(chunk_used, 2)
                for g in range(0 if h0 is None else 2, 4):
                    pe.wait_ge(tile_taken, T0 + 4 * i + g - 3)
                    for k in range(KT):
                        e = 2 * g + k // 8
                        if k % 8 == 0:
                            pe.wait_ge(lo_done, c0 + 8 * i + e + 1)
                        mm = product(bank[(T0 + g) % 4][:, 0:SEQ], (c0 + e) % RING, k % 8, h_hi[:, k, :],
                                     h_lo[:, k, :], k == 0, k == KT - 1)
                        if k % 8 == 7:
                            mm.then_inc(chunk_used, 1)

            def ffn(c0, T0, P0, Y0, h0, layer):
                pe.wait_ge(tile_taken, T0 - 2)
                up(c0, T0, 0, h0)
                with pe.Fori(1, PARTS[0] // 2) as i:
                    up(c0, T0, i)
                ada_sum(B_UP1 if layer else B_UP0)
                c1 = c0 + 4 * PARTS[0]
                with pe.Fori(0, KT // 2) as i:
                    for t in range(2):
                        pe.wait_ge(y_free, Y0 + 2 * i + t + 1)
                        for k in range(PARTS[0]):
                            e = 4 * t + k // 8
                            if k % 8 == 0:
                                pe.wait_ge(lo_done, c1 + 8 * i + e + 1)
                                pe.wait_ge(a_ready, P0 + k + 8)
                            mm = product(bank[4 + t][:, 0:SEQ], (c1 + e) % RING, k % 8, a_hi[:, k, :], a_lo[:, k, :],
                                         k == 0, k == PARTS[0] - 1)
                            if k % 8 == 7:
                                mm.then_inc(chunk_used, 1)
                if layer == 0:
                    ada_sum(B_DOWN0)
                c2 = c1 + 2 * PARTS[0]
                with pe.Fori(0, PARTS[1] // 2) as i:
                    up(c2, T0 + 2 * PARTS[0], i)
                c3 = c2 + 4 * PARTS[1]
                for t in range(KT):
                    pe.wait_ge(y_free, Y0 + KT + t + 1)
                    for k in range(PARTS[1]):
                        u = PARTS[1] * t + k
                        c = c3 + u // 8
                        if u % 8 == 0:
                            pe.wait_ge(lo_done, c + 1)
                        if t == 0:
                            pe.wait_ge(a_ready, P0 + PARTS[0] + k + 1)
                        mm = product(bank[4 + t % 2][:, 0:SEQ], c % RING, u % 8, a_hi[:, k, :], a_lo[:, k, :],
                                     k == 0, k == PARTS[1] - 1)
                        if u % 8 == 7:
                            mm.then_inc(chunk_used, 1)
                    if t % 2 == 0:
                        mm.then_inc(y_done, 1)

            pe.wait_ge(o_taken, 1 + HEADS)
            square(C_WO, Y_WO, h_hi, h_lo)
            residual_sum(0)
            ada_sum(B_WO)
            ffn(C_FFN0, T_UP0, 0, Y_FFN0, H_L0F, 0)
            residual_sum(1)
            ada_sum(B_PART0)

            def spectrum(g):
                for t in range(2):
                    if g:
                        pe.wait_ge(ab_ready, 2 * g - 1 + t)
                    for k in range(2):
                        tok = slice(t * P, (t + 1) * P)
                        m = 2 * g + k
                        pe.wait_ge(h_ready, H_L1 + m + 1)
                        mm = moving(bank[4 + t][:, :], h_hi[:, m, tok], h_lo[:, m, tok], dft_hi[:, k, 0:2 * SEQ],
                                    dft_lo[:, k, 0:2 * SEQ], k == 0, k == 1)
                    mm.then_inc(ab_done, 1)

            def back(g):
                for m in range(2):
                    T = T_DFT + 2 * g + m
                    pe.wait_ge(tile_taken, T - 3)
                    pe.wait_ge(ab_ready, 2 * g + 2)
                    for n, (t, part, table) in enumerate(((0, 0, 0), (1, 0, 0), (0, SEQ, 2 * SEQ), (1, SEQ, 2 * SEQ))):
                        ch = slice(part + m * P, part + (m + 1) * P)
                        to = slice(table, table + SEQ)
                        mm = moving(bank[T % 4][:, 0:SEQ], ab_hi[:, g % 2, t, ch], ab_lo[:, g % 2, t, ch],
                                    dft_hi[:, t, to], dft_lo[:, t, to], n == 0, n == 3)
                    mm.then_inc(tile_done, 1)

            pe.wait_ge(dft_ready, 1)
            for g in range(9):
                if g < 8:
                    spectrum(g)
                if g:
                    back(g - 1)
            pe.wait_ge(tile_taken, T_UP1)
            square(C_FNO, Y_FNO, f_hi, f_lo)
            residual_sum(2)
            ada_sum(B_FNO)
            ffn(C_FFN1, T_UP1, FT, Y_FFN1, H_L1F, 1)
            residual_sum(3)


def tile_blocks(w):
    k, m = w.shape
    return w.reshape(k // P, P, m // P, P).transpose(2, 0, 1, 3)


def as_chunks(blocks):
    return blocks.reshape(-1, 8, P, P).transpose(0, 2, 1, 3).reshape(-1, P, CH)


def weight_stream(w_dqkv, w_uq, w_ukv, w_o, fno_w, w_up, w_down):
    out = np.empty((N_CHUNKS, P, CH), np.float32)
    at = [0]

    def put(chunks):
        out[at[0]:at[0] + len(chunks)] = chunks
        at[0] += len(chunks)

    put(as_chunks(tile_blocks(w_dqkv[:, LORA:2 * LORA])))
    kr = w_dqkv[:, 2 * LORA:]
    put(as_chunks(tile_blocks(np.concatenate([kr, kr], 1))))
    put(as_chunks(tile_blocks(w_dqkv[:, :LORA])))
    q = w_uq.reshape(LORA, HEADS, P + ROPE)
    kv = w_ukv.reshape(LORA, HEADS, P + VD)

    def kq(h):
        return as_chunks(np.concatenate([tile_blocks(kv[:, h, :P])[0], tile_blocks(q[:, h, :P])[0]]))

    def values(p):
        w = kv[:, 2 * p:2 * p + 2, P:].reshape(LT, P, 2 * VD)
        return w.transpose(1, 0, 2).reshape(1, P, CH)

    def rope_q(p):
        w = np.zeros((8, P, P), np.float32)
        w[:LT] = tile_blocks(q[:, 2 * p:2 * p + 2, P:].reshape(LORA, P))[0]
        return as_chunks(w)

    put(values(0))
    put(rope_q(0))
    put(kq(0))
    for n in range(HEADS - 1):
        if n % 2:
            put(rope_q(n // 2 + 1))
        put(kq(n + 1))
        if n % 2 == 0 and n < HEADS - 2:
            put(values(n // 2 + 1))
    put(as_chunks(tile_blocks(w_o)))
    for layer in range(2):
        if layer:
            put(as_chunks(tile_blocks(fno_w)))
        up = tile_blocks(w_up[layer])
        up = np.stack([up[:FT], up[FT:]], 1)
        down = tile_blocks(w_down[layer])
        lo = 0
        for n in PARTS:
            put(as_chunks(up[lo:lo + n]))
            put(as_chunks(down[:, lo:lo + n]))
            lo += n
    assert at[0] == N_CHUNKS
    return out


def constants():
    ident_ones = np.stack([np.eye(P), np.ones((P, P))], 1).astype(np.float32)
    half = ROPE // 2
    inv = np.power(np.float32(10000.0), -np.arange(0, half, 2, dtype=np.float32) / np.float32(half))
    pos = np.arange(SEQ)
    ang_r = (pos // GRID_W).astype(np.float32)[:, None] * inv
    ang_c = (pos % GRID_W).astype(np.float32)[:, None] * inv
    ang = np.concatenate([ang_r, ang_r, ang_c, ang_c], -1).T
    ang = np.concatenate([ang, ang], 0)
    turn = np.zeros((P, P), np.float32)
    for b in range(0, P, half):
        for j in range(half // 2):
            turn[b + half // 2 + j, b + j] = -1.0
            turn[b + j, b + half // 2 + j] = 1.0
    pairing = np.zeros((P, 2))
    pairing[[0, 1, 2, 3], [0, 1, 0, 1]] = 1.0
    rope = np.concatenate([np.cos(ang), np.sin(ang), turn, pairing], 1).astype(np.float32)
    nk = np.outer(np.arange(SEQ), np.arange(SEQ)) % SEQ
    c, s = np.cos(2 * np.pi * nk / SEQ) / 16, np.sin(2 * np.pi * nk / SEQ) / 16
    dft = np.concatenate([c, s, -s], 1).reshape(2, P, 3 * SEQ).transpose(1, 0, 2).astype(np.float32)
    return ident_ones, rope, dft


def kernel(**inputs):
    import numpy as _np
    import concourse.bacc as _bacc
    from concourse import mybir as _mybir
    from concourse.bass_utils import run_bass_kernel_spmd as _run

    g = {k: _np.asarray(v) for k, v in inputs.items()}

    def columns(v):
        return _np.moveaxis(v.reshape(v.shape[:-1] + (-1, P)), -1, 0)

    ident_ones, rope, dft = constants()
    aw = g["ada_w"].reshape(2, D, 6, D)
    rows = aw.reshape(2, KT, P, 6, 2, CH).transpose(0, 3, 1, 4, 2, 5).reshape(12, KT, 2, P, CH)
    early = rows[0:2].transpose(0, 2, 1, 3, 4).reshape(N_EARLY, P, CH)
    late = _np.empty((N_ADA, P, CH), _np.float32)
    for b, (first, n) in enumerate(ADA_BLOCKS):
        late[ADA_AT[b]:ADA_AT[b + 1]] = rows[first:first + n].transpose(1, 0, 2, 3, 4).reshape(-1, P, CH)
    conv = _np.concatenate([g["ffn_conv_w"], g["ffn_conv_b"][:, None]], 1)
    conv = conv.reshape(2, 4, 2, FT, P).transpose(0, 4, 3, 2, 1).reshape(2, P, 2 * FT, 4)
    arrays = {
        "xT": columns(g["x"][0]).transpose(0, 2, 1),
        "ctxT": columns(g["ctx"][0]).transpose(0, 2, 1),
        "cond": columns(_np.stack([g["c"][0], g["c_ctx"]])).transpose(0, 2, 1),
        "ada_early": early,
        "ada_late": late,
        "ada_b": columns(g["ada_b"].reshape(12, D)),
        "gains": columns(_np.concatenate([g["norm1_g"], g["norm2_g"], g["final_norm_g"][None]])),
        "lat_gains": columns(_np.concatenate([g["mla_q_norm_g"], g["mla_kv_norm_g"]])),
        "weights": weight_stream(g["mla_w_dqkv"][0], g["mla_w_uq"][0], g["mla_w_ukv"][0], g["mla_w_o"][0],
                                 g["fno_w"][0], g["ffn_w_up"], g["ffn_w_down"]),
        "conv": conv,
        "consts": ident_ones,
        "rope": rope,
        "dft": dft,
    }
    nc = _bacc.Bacc("TRN2", target_bir_lowering=False, num_devices=1)
    args = []
    for name, a in arrays.items():
        arrays[name] = a = _np.ascontiguousarray(a)
        args.append(nc.dram_tensor(name, a.shape, _mybir.dt.from_np(a.dtype), kind="ExternalInput").ap())
    out = nc.dram_tensor("outT", (P, KT, SEQ), _mybir.dt.float32, kind="ExternalOutput").ap()
    backbone(nc, *args, out)
    r = _run(nc, [arrays], core_ids=[0])
    got = r.results[0]["outT"]
    return _np.ascontiguousarray(got.transpose(2, 1, 0)).reshape(1, SEQ, D)
```
